# Optimizing a Trainium2 kernel written in Bass

```python
import jax, jax.numpy as jnp
from jax import lax
import numpy as np

D_MODEL = 1024
BATCH = 1
SEQ = 256
DEPTH = 2

CHUNK = 64
PLE_DIM = 256
HEAD_DIM = 64
D_POOL = D_MODEL // 4
D_SB = (D_MODEL - D_POOL) // 2
D_LRU = D_MODEL - D_POOL - D_SB
D_MIX = D_SB + D_LRU + D_POOL
SB_HEADS = D_SB // HEAD_DIM
LRU_HEADS = D_LRU // HEAD_DIM
POOL_WINDOWS = (2, 4, 8, 16)
POOL_GROUP = D_POOL // len(POOL_WINDOWS)
D_IN = 3 * D_SB + 2 * D_LRU + D_POOL
CONV_WIDTH = 4
LRU_C = 8.0
D_FF = ((8 * D_MODEL // 3 + 127) // 128) * 128
Q_BLOCK = 128
EPS = 1e-6

kernel_name = 'hybrid_sb_lru_pool_macaron'

def rms_norm(x, g):
    xf = x.astype(jnp.float32)
    y = xf * lax.rsqrt(jnp.mean(xf * xf, axis=-1, keepdims=True) + EPS)
    return (y * g.astype(jnp.float32)).astype(x.dtype)

def swiglu_ffn(x, g, w1, w3, w2):
    h = rms_norm(x, g)
    return (jax.nn.silu(h @ w1) * (h @ w3)) @ w2

def stick_breaking_attention(q, k, v):
    b, s, h, dh = q.shape
    nb = s // Q_BLOCK
    scale = dh ** -0.5
    kt = k.transpose(0, 2, 1, 3)
    vt = v.transpose(0, 2, 1, 3)
    qb = q.reshape(b, nb, Q_BLOCK, h, dh).transpose(1, 0, 3, 2, 4)
    q_pos = jnp.arange(s, dtype=jnp.int32).reshape(nb, Q_BLOCK)
    k_pos = jnp.arange(s, dtype=jnp.int32)

    def block(args):
        q_blk, pos = args
        z = jnp.einsum('bhqd,bhkd->bhqk', q_blk, kt).astype(jnp.float32) * scale
        mask = k_pos[None, :] < pos[:, None]
        log_beta = jax.nn.log_sigmoid(z)
        log_keep = jnp.where(mask, log_beta - z, 0.0)
        suffix = lax.cumsum(log_keep, axis=3, reverse=True) - log_keep
        w = jnp.where(mask, jnp.exp(log_beta + suffix), 0.0)
        return jnp.einsum('bhqk,bhkd->bhqd', w.astype(vt.dtype), vt)

    o = lax.map(block, (qb, q_pos))
    return o.transpose(1, 0, 3, 2, 4).reshape(b, s, h * dh)

def rg_lru_branch(xb, gate, conv_w, conv_b, wa, ba, wx, bx, lam):
    b, s, d = xb.shape
    xc = lax.conv_general_dilated(
        xb, conv_w[:, None, :], window_strides=(1,), padding=[(CONV_WIDTH - 1, 0)],
        dimension_numbers=('NWC', 'WIO', 'NWC'), feature_group_count=d) + conv_b
    xh = xc.reshape(b, s, LRU_HEADS, d // LRU_HEADS)
    r = jax.nn.sigmoid(jnp.einsum('bshi,hij->bshj', xh, wa).reshape(b, s, d) + ba)
    i = jax.nn.sigmoid(jnp.einsum('bshi,hij->bshj', xh, wx).reshape(b, s, d) + bx)
    log_a = (-LRU_C * r.astype(jnp.float32)) * jax.nn.softplus(-lam.astype(jnp.float32))
    a = jnp.exp(log_a)
    u = jnp.sqrt(-jnp.expm1(2.0 * log_a)) * (i * xc).astype(jnp.float32)

    def combine(left, right):
        a_l, b_l = left
        a_r, b_r = right
        return a_l * a_r, a_r * b_l + b_r

    _, h = lax.associative_scan(combine, (a, u), axis=1)
    return jax.nn.gelu(gate) * h.astype(xb.dtype)

def multiscale_pool(xc, pool_w, pool_scale):
    b, s, d = xc.shape
    xf = xc.astype(jnp.float32)
    count = jnp.arange(1, s + 1, dtype=jnp.float32)[None, :, None]
    outs = []
    for g, w in enumerate(POOL_WINDOWS):
        xg = xf[..., g * POOL_GROUP:(g + 1) * POOL_GROUP]
        cs = jnp.cumsum(xg, axis=1)
        prev = jnp.pad(cs, ((0, 0), (w, 0), (0, 0)))[:, :s]
        mean = (cs - prev) / jnp.minimum(count, float(w))
        outs.append(mean - xg)
    pooled = jnp.stack(outs, axis=2).astype(xc.dtype)
    y = jnp.einsum('bsgi,gij->bsgj', pooled, pool_w).reshape(b, s, d)
    return y * pool_scale

def setup_inputs(seed: int = 0) -> dict:
    key = jax.random.key(seed)
    ks = iter(jax.random.split(key, 40))

    def w(shape, fan_in):
        return jax.random.normal(next(ks), shape, jnp.float32) * (fan_in ** -0.5)

    def gain(shape):
        return 1.0 + 0.02 * jax.random.normal(next(ks), shape, jnp.float32)

    def bias(shape):
        return 0.02 * jax.random.normal(next(ks), shape, jnp.float32)

    x = jax.random.normal(next(ks), (BATCH, SEQ, D_MODEL), jnp.float32)
    p = jax.random.normal(next(ks), (DEPTH, BATCH, SEQ, PLE_DIM), jnp.float32)
    u = jax.random.uniform(next(ks), (DEPTH, D_LRU), jnp.float32, minval=0.9, maxval=0.999)
    a0 = u ** (1.0 / LRU_C)
    lru_lambda = jnp.log(a0) - jnp.log1p(-a0)
    gh = D_LRU // LRU_HEADS
    return {
        'x': x,
        'p': p,
        'ffn1_norm': gain((DEPTH, D_MODEL)),
        'ffn1_w1': w((DEPTH, D_MODEL, D_FF), D_MODEL),
        'ffn1_w3': w((DEPTH, D_MODEL, D_FF), D_MODEL),
        'ffn1_w2': w((DEPTH, D_FF, D_MODEL), D_FF),
        'mix_norm': gain((DEPTH, D_MODEL)),
        'w_in': w((DEPTH, D_MODEL, D_IN), D_MODEL),
        'q_norm': gain((DEPTH, HEAD_DIM)),
        'k_norm': gain((DEPTH, HEAD_DIM)),
        'conv_w': w((DEPTH, CONV_WIDTH, D_LRU), CONV_WIDTH),
        'conv_b': bias((DEPTH, D_LRU)),
        'lru_wa': w((DEPTH, LRU_HEADS, gh, gh), gh),
        'lru_ba': bias((DEPTH, D_LRU)),
        'lru_wx': w((DEPTH, LRU_HEADS, gh, gh), gh),
        'lru_bx': bias((DEPTH, D_LRU)),
        'lru_lambda': lru_lambda,
        'pool_w': w((DEPTH, len(POOL_WINDOWS), POOL_GROUP, POOL_GROUP), POOL_GROUP),
        'pool_scale': 1.0 + 0.1 * jax.random.normal(next(ks), (DEPTH, D_POOL), jnp.float32),
        'w_out': w((DEPTH, D_MIX, D_MODEL), D_MIX),
        'ffn2_norm': gain((DEPTH, D_MODEL)),
        'ffn2_w1': w((DEPTH, D_MODEL, D_FF), D_MODEL),
        'ffn2_w3': w((DEPTH, D_MODEL, D_FF), D_MODEL),
        'ffn2_w2': w((DEPTH, D_FF, D_MODEL), D_FF),
        'ple_norm': gain((DEPTH, D_MODEL)),
        'ple_gate_w': w((DEPTH, D_MODEL, D_MODEL), D_MODEL),
        'ple_proj': w((DEPTH, PLE_DIM, D_MODEL), PLE_DIM),
    }

def reference(x, p, ffn1_norm, ffn1_w1, ffn1_w3, ffn1_w2, mix_norm, w_in, q_norm, k_norm,
              conv_w, conv_b, lru_wa, lru_ba, lru_wx, lru_bx, lru_lambda, pool_w, pool_scale,
              w_out, ffn2_norm, ffn2_w1, ffn2_w3, ffn2_w2, ple_norm, ple_gate_w, ple_proj):
    b, s, _ = x.shape
    splits = [D_SB, 2 * D_SB, 3 * D_SB, 3 * D_SB + D_LRU, 3 * D_SB + 2 * D_LRU]
    for i in range(DEPTH):
        x = x + 0.5 * swiglu_ffn(x, ffn1_norm[i], ffn1_w1[i], ffn1_w3[i], ffn1_w2[i])
        h = rms_norm(x, mix_norm[i])
        proj = h @ w_in[i]
        q, k, v, xb, gb, xc = jnp.split(proj, splits, axis=-1)
        q = rms_norm(q.reshape(b, s, SB_HEADS, HEAD_DIM), q_norm[i])
        k = rms_norm(k.reshape(b, s, SB_HEADS, HEAD_DIM), k_norm[i])
        v = v.reshape(b, s, SB_HEADS, HEAD_DIM)
        o_sb = stick_breaking_attention(q, k, v)
        o_lru = rg_lru_branch(xb, gb, conv_w[i], conv_b[i], lru_wa[i], lru_ba[i],
                              lru_wx[i], lru_bx[i], lru_lambda[i])
        o_pool = multiscale_pool(xc, pool_w[i], pool_scale[i])
        x = x + jnp.concatenate([o_sb, o_lru, o_pool], axis=-1) @ w_out[i]
        x = x + 0.5 * swiglu_ffn(x, ffn2_norm[i], ffn2_w1[i], ffn2_w3[i], ffn2_w2[i])
        gate = jax.nn.sigmoid(rms_norm(x, ple_norm[i]) @ ple_gate_w[i])
        x = x + gate * (p[i] @ ple_proj[i])
    return x


_drawn_inputs = setup_inputs


def setup_inputs(seed=0):
    import zlib

    import numpy as np

    out = dict(_drawn_inputs(seed))
    spreads = {}
    factors = {'ffn1_norm': 5.657,
     'mix_norm': 3.826,
     'q_norm': 8.0,
     'k_norm': 8.0,
     'lru_ba': 26.149,
     'lru_bx': 8.0,
     'ffn2_norm': 6.857,
     'ple_norm': 64.0,
     'conv_b': 3.144}
    for name, (base, spread) in spreads.items():
        noise = np.random.default_rng([zlib.crc32(name.encode()), seed]).standard_normal(out[name].shape)
        drawn = base * np.exp(spread * noise) if base else spread * noise
        out[name] = __import__('jax').numpy.asarray(drawn.astype(out[name].dtype))
    for name, factor in factors.items():
        out[name] = (out[name] * factor).astype(out[name].dtype)
    return out
```

```python
from contextlib import ExitStack

import numpy as np

import concourse.bass as bass
from concourse import mybir

P = 128
F32 = mybir.dt.float32
F32R = mybir.dt.float32r
I32 = mybir.dt.int32
ALU = mybir.AluOpType
ACT = mybir.ActivationFunctionType

RING = 3
HALVES = 2
UNIT = 2048
EPS = 1e-6
BANK = 512
WINDOWS = (2, 4, 8, 16)


class Steps:

    def __init__(self, engine, semaphore, per_layer):
        self.engine, self.semaphore, self.per_layer = engine, semaphore, per_layer
        self.base, self.count = 0, 0

    def start_layer(self, layer):
        self.base, self.count = layer * self.per_layer, 0

    def done(self, instruction):
        instruction.then_inc(self.semaphore, 1)
        self.count += 1

    def settle(self):
        self.engine.wait_ge(self.semaphore, self.base + self.count)

    def end_layer(self):
        assert self.count == self.per_layer, (self.semaphore, self.count)


def trunk_kernel(nc, x_in, p_in, ffn1_norm, ffn1_w1, ffn1_w3, ffn1_w2, mix_norm, w_in, q_norm, k_norm,
                 conv_w, conv_b, lru_wa, lru_ba, lru_wx, lru_bx, lru_lambda, pool_w, pool_scale,
                 w_out, ffn2_norm, ffn2_w1, ffn2_w3, ffn2_w2, ple_norm, ple_gate_w, ple_proj, out):
    DEPTH, D, FF = ffn1_w1.shape
    SEQ = x_in.shape[1]
    T = SEQ // P
    KC = D // P
    DH = q_norm.shape[1]
    PLE = ple_proj.shape[1]
    TAPS, D_LRU = conv_w.shape[1:]
    D_POOL = pool_scale.shape[1]
    D_SB = D - D_POOL - D_LRU
    HEADS = D_SB // DH
    LC = D_LRU // P
    GROUP = 256
    GROUPS = FF // GROUP
    assert (SEQ, D, DH, PLE, D_SB, D_LRU, D_POOL, TAPS) == (256, 1024, 64, 256, 384, 384, 256, 4)
    assert FF % GROUP == 0 and T == 2

    FFN_UNITS = 3 * GROUPS
    U_FFN1 = 0
    U_MIX = U_FFN1 + FFN_UNITS
    MIX_UNITS = 13
    U_FFN2 = U_MIX + MIX_UNITS
    U_PLE = U_FFN2 + FFN_UNITS
    PLE_UNITS = 5
    UNITS = U_PLE + PLE_UNITS
    assert UNITS % RING == 0
    USES = UNITS // RING

    ROW_CONV_W = 0
    ROW_CONV_B = ROW_CONV_W + TAPS * LC
    ROW_BA = ROW_CONV_B + LC
    ROW_BX = ROW_BA + LC
    ROW_LAM = ROW_BX + LC
    ROW_SCALE = ROW_LAM + LC
    ROW_QN = ROW_SCALE + D_POOL // P
    ROW_KN = ROW_QN + 1
    ROWS = ROW_KN + 1
    PARAM_DMAS = 10 + 6

    with ExitStack() as ctx:
        def sb(name, shape, dt=F32):
            return ctx.enter_context(nc.sbuf_tensor(name, shape, dt))

        def sem(name):
            return ctx.enter_context(nc.semaphore(name))

        raw = [sb(f"raw{s}", [P, UNIT]) for s in range(RING)]
        whi = [sb(f"w_hi{s}", [P, UNIT], F32R) for s in range(RING)]
        wlo = [sb(f"w_lo{s}", [P, UNIT], F32R) for s in range(RING)]
        x = sb("x", [P, T, D])
        xg = sb("x_gained", [P, T, D])
        xt_hi = sb("xt_hi", [P, KC, SEQ], F32R)
        xt_lo = sb("xt_lo", [P, KC, SEQ], F32R)
        scratch = sb("scratch", [P, 4, BANK])
        gain = [sb(f"gain{i}", [P, D]) for i in range(2)]
        square_sums = sb("square_sums", [P, 4])
        mean_sq = sb("mean_sq", [P, T])
        rms = sb("rms", [P, T])
        rstd = sb("rstd", [P, T])
        ident = sb("ident", [P, P])
        ones = sb("ones", [P, P])
        neg_ones = sb("neg_ones", [P, P])
        neg_later = sb("neg_later", [P, P])
        causal = sb("causal", [P, P])
        head_mean = sb("head_mean", [P, P])
        eps_col = sb("eps_col", [P, 1])
        inv_count = sb("inv_count", [P, 2, SEQ])
        silu = sb("silu", [P, T, GROUP])
        gated = sb("gated", [P, T, GROUP])
        gt_hi = sb("gt_hi", [P, 2, T, P], F32R)
        gt_lo = sb("gt_lo", [P, 2, T, P], F32R)
        param_rows = sb("param_rows", [P, P])
        par = sb("param_cols", [P, ROWS])
        tiny = sb("tiny", [P, 8, LC])
        decay_scale = sb("decay_scale", [P, LC])
        qk_gain = sb("qk_gain", [P, 1])
        diag = sb("diag_rstd", [P, SEQ])
        rrow = sb("rstd_rows", [P, SEQ])
        qk = sb("qk", [P, 6, SEQ])
        qk_sq = xg[:, :, :].rearrange("p t d -> p (t d)")[:, 0:6 * SEQ].rearrange("p (c n) -> p c n", c=6)
        v = sb("v", [P, T, D_SB])
        HB = 3
        logs = [sb(f"logs{i}", [P, 3 * P]) for i in range(HB)]
        soft = [sb(f"soft{i}", [P, 3 * P]) for i in range(HB)]
        lbeta = [sb(f"lbeta{i}", [P, 3 * P]) for i in range(HB)]
        xpad = sb("xb_padded", [P, LC, TAPS - 1 + SEQ])
        xconv = sb("xconv", [P, LC, SEQ])
        gb = sb("gb", [P, LC, SEQ])
        gates = scratch[:, :, :].rearrange("p q n -> p (q n)")[:, 0:2 * D_LRU // P * SEQ] \
            .rearrange("p (g c n) -> p g c n", g=2, c=LC)
        r_gate, i_gate = gates[:, 0], gates[:, 1]
        th = sb("tanh_half", [P, LC, SEQ])
        rec = sb("rec", [P, LC, SEQ])
        decay = sb("decay", [P, LC, SEQ])
        PADW = max(WINDOWS)
        xc_pad = sb("xc_padded", [P, 2, PADW + SEQ])
        sums = [sb(f"sum{w}", [P, 2, PADW + SEQ]) for w in WINDOWS[:2]]
        sums += [sb(f"sum{w}", [P, 1, PADW + SEQ]) for w in WINDOWS[2:]]
        pooled = sb("pooled", [P, 2, SEQ])
        count_i = pooled[:, :, :].bitcast(I32)
        bd_a = sb("bd_a", [P, LC, P])
        bd_x = sb("bd_x", [P, LC, P])
        bd_p = sb("bd_p", [P, 2, P])
        mix_hi = sb("mix_hi", [P, KC, SEQ], F32R)
        mix_lo = sb("mix_lo", [P, KC, SEQ], F32R)
        pl = qk[:, 0:T, :]
        pt_hi, pt_lo = mix_hi[:, 0:PLE // P, :], mix_lo[:, 0:PLE // P, :]

        acc = [ctx.enter_context(nc.psum_tensor(f"acc{i}", [P, BANK], F32)) for i in range(4)]
        up = [ctx.enter_context(nc.psum_tensor(f"up{i}", [P, BANK], F32)) for i in range(T)]
        turn = [ctx.enter_context(nc.psum_tensor(f"turn{i}", [P, BANK], F32)) for i in range(2)]

        slot_loaded = [sem(f"slot_loaded{s}") for s in range(RING)]
        hi_split = sem("hi_split")
        lo_split = sem("lo_split")
        unit_used = sem("unit_used")
        x_loaded = sem("x_loaded")
        gain_loaded = [sem(f"gain_loaded{i}") for i in range(2)]
        params_loaded = sem("params_loaded")
        p_loaded = sem("p_loaded")
        consts_ready = sem("consts_ready")
        pool_step = sem("pool_step")
        dve_step = sem("dve_step")
        act_step = sem("act_step")
        acc_ready = sem("acc_ready")
        gained = sem("gained")
        xt_turned = sem("xt_turned")
        xt_rounded = sem("xt_rounded")
        xt_split = sem("xt_split")
        squares_summed = sem("squares_summed")
        mean_ready = sem("mean_ready")
        rms_ready = sem("rms_ready")
        rstd_ready = sem("rstd_ready")
        up_ready = sem("up_ready")
        silu_ready = sem("silu_ready")
        gated_ready = sem("gated_ready")
        g_turned = sem("g_turned")
        gt_rounded = sem("gt_rounded")
        gt_split = sem("gt_split")
        params_turned = sem("params_turned")
        params_ready = sem("params_ready")
        lam_exp_ready = sem("lam_exp_ready")
        diag_ready = sem("diag_ready")
        rrow_turned = sem("rrow_turned")
        rrow_ready = sem("rrow_ready")
        qk_scaled = sem("qk_scaled")
        qk_squared = sem("qk_squared")
        qk_summed = sem("qk_summed")
        qk_rstd = sem("qk_rstd")
        qk_normed = sem("qk_normed")
        v_ready = sem("v_ready")
        z_ready = sem("z_ready")
        log_ready = sem("log_ready")
        keep_ready = sem("keep_ready")
        suffix_ready = sem("suffix_ready")
        logw_ready = sem("logw_ready")
        w_exped = sem("w_exped")
        w_ready = sem("w_ready")
        o_ready = sem("o_ready")
        o_rounded = sem("o_rounded")
        att_split = sem("att_split")
        evacuated = sem("evacuated")
        conv_ready = sem("conv_ready")
        gates_product = sem("gates_product")
        tanh_ready = sem("tanh_ready")
        root_ready = sem("root_ready")
        gelu_ready = sem("gelu_ready")
        lru_ready = sem("lru_ready")
        lru_rounded = sem("lru_rounded")
        lru_split = sem("lru_split")
        pooled_ready = sem("pooled_ready")
        pool_product = sem("pool_product")
        pool_rounded = sem("pool_rounded")
        pool_split = sem("pool_split")
        p_turned = sem("p_turned")
        p_rounded = sem("p_rounded")
        p_split = sem("p_split")
        sig_ready = sem("sig_ready")
        decay_ready = sem("decay_ready")
        inverse_ready = sem("inverse_ready")
        x_done = sem("x_done")
        stored = sem("stored")

        block = ctx.enter_context(nc.Block())

        def unit_count(layer, offset, j=0):
            return layer * UNITS + offset + RING * j + 1

        def slot_use(layer, offset, j=0):
            return layer * USES + offset // RING + j + 1

        def wait_unit(engine, layer, offset, j=0):
            engine.wait_ge(unit_used, unit_count(layer, offset, j) + RING)

        def wait_quarter(engine, layer, i, q, last_unit):
            if q < 3:
                engine.wait_ge(acc_ready, layer * 12 + 3 * i + q + 1)
            else:
                wait_unit(engine, layer, last_unit)

        def up_product_ready(engine, layer, f, base, j, t):
            if t == 0:
                engine.wait_ge(up_ready, layer * 2 * GROUPS + f * GROUPS + j + 1)
            else:
                wait_unit(engine, layer, base + (1 if isinstance(j, int) else 0),
                          0 if isinstance(j, int) else j)

        PHASE_ENDS = (U_MIX - 1, U_FFN2 - 1, U_PLE - 1, UNITS - 1)
        head_bank = [up[0], up[1], turn[1]]
        proj_bank = [up[0], up[1], turn[0], turn[1]]
        ACT_STEPS, DVE_STEPS, CONSTS = 20, 59, 28

        @block.sync
        def _(sp):
            sp.dma_start(x[:, :, :], x_in[0].rearrange("(t p) d -> p t d", p=P)).then_inc(x_loaded, 16)

            def load(layer, offset, parts, j=0):
                sp.wait_ge(lo_split, unit_count(layer, offset, j))
                for dst, src in parts:
                    sp.dma_start(dst, src).then_inc(slot_loaded[offset % RING], 16)

            def load_up(layer, offset, half, g, w1, w3, j=0):
                ks = slice(4 * half, 4 * half + 4)
                dst = raw[offset % RING][:, :].rearrange("p (k m n) -> p k m n", k=4, m=2)
                load(layer, offset, [
                    (dst[:, :, m, :], w.rearrange("l (k p) f -> l p k f", p=P)[layer, :, ks, bass.ts(g, GROUP)])
                    for m, w in enumerate((w1, w3))], j)

            def load_rows(layer, offset, w, row0, j=0):
                dst = raw[offset % RING][:, :].rearrange("p (c n) -> p c n", c=2)
                src = w.rearrange("l (r c p) n -> l r p c n", c=2, p=P)
                load(layer, offset, [(dst[:, c, :], src[layer, row0, :, c, :]) for c in (1, 0)], j)

            def load_cols(layer, offset, col0):
                dst = raw[offset % RING][:, :].rearrange("p (k n) -> p k n", k=KC)
                src = w_in.rearrange("l (k p) n -> l p k n", p=P)
                load(layer, offset, [(dst[:, k:k + 4, :], src[layer, :, k:k + 4, col0:col0 + 256])
                                     for k in (0, 4)])

            def load_v(layer, offset, half):
                dst = raw[offset % RING][:, 0:4 * D_SB].rearrange("p (k n) -> p k n", k=4)
                src = w_in.rearrange("l (k p) n -> l p k n", p=P)
                load(layer, offset, [(dst[:, k:k + 2, :],
                                      src[layer, :, 4 * half + k:4 * half + k + 2, 2 * D_SB:3 * D_SB])
                                     for k in (0, 2)])

            def load_gain(layer, i, source):
                sp.dma_start(gain[i % 2][:, :], source[bass.ds(layer, 1), :].to_broadcast([P, D])
                             ).then_inc(gain_loaded[i % 2], 16)

            def load_params(layer):
                for row, src in (
                    (ROW_CONV_W, conv_w.rearrange("l w (c p) -> l (w c) p", p=P)),
                    (ROW_CONV_B, conv_b.rearrange("l (c p) -> l c p", p=P)),
                    (ROW_BA, lru_ba.rearrange("l (c p) -> l c p", p=P)),
                    (ROW_BX, lru_bx.rearrange("l (c p) -> l c p", p=P)),
                    (ROW_LAM, lru_lambda.rearrange("l (c p) -> l c p", p=P)),
                    (ROW_SCALE, pool_scale.rearrange("l (c p) -> l c p", p=P)),
                ):
                    sp.dma_start(param_rows[row:row + src.shape[1], :], src[layer]).then_inc(params_loaded, 16)
                for row, src in ((ROW_QN, q_norm), (ROW_KN, k_norm)):
                    for b in range(2):
                        sp.dma_start(param_rows[row:row + 1, b * DH:(b + 1) * DH],
                                     src[bass.ds(layer, 1), :]).then_inc(params_loaded, 16)
                for bd, src in ((bd_a, lru_wa), (bd_x, lru_wx), (bd_p, pool_w)):
                    for b in range(2):
                        blk = slice(b * DH, (b + 1) * DH)
                        sp.dma_start(bd[blk, :, blk], src.rearrange("l (c b) i j -> l b i c j", b=2)[layer, b]
                                     ).then_inc(params_loaded, 16)

            def load_ffn(layer, base, w1, w3, w2, after_first, before_last):
                load_up(layer, base, 0, 0, w1, w3)
                load_up(layer, base + 1, 1, 0, w1, w3)
                after_first()
                with sp.Fori(1, GROUPS) as j:
                    load_up(layer, base - 1, 0, j, w1, w3, j)
                    load_up(layer, base, 1, j, w1, w3, j)
                    load_rows(layer, base + 1, w2, j - 1, j)
                before_last()
                load_rows(layer, base - 1, w2, GROUPS - 1, GROUPS)

            sp.wait_ge(consts_ready, CONSTS)
            with sp.Fori(0, DEPTH) as layer:
                def first_gains():
                    load_gain(layer, 0, ffn1_norm)
                    load_gain(layer, 1, mix_norm)

                def embeddings():
                    sp.dma_start(pl[:, :, :], p_in.rearrange("l b (t p) e -> l p (b t) e", p=P)[layer]
                                 ).then_inc(p_loaded, 16)

                load_ffn(layer, U_FFN1, ffn1_w1, ffn1_w3, ffn1_w2, first_gains, lambda: load_params(layer))
                load_gain(layer, 2, ffn2_norm)
                for n in range(3):
                    load_cols(layer, U_MIX + n, 256 * n)
                for n in range(2):
                    load_v(layer, U_MIX + 3 + n, n)
                for n in range(4):
                    load_cols(layer, U_MIX + 5 + n, 3 * D_SB + 256 * n)
                for n, row in enumerate((3, 0, 1, 2)):
                    load_rows(layer, U_MIX + 9 + n, w_out, row)
                load_gain(layer, 3, ple_norm)
                load_ffn(layer, U_FFN2, ffn2_w1, ffn2_w3, ffn2_w2, lambda: None, embeddings)
                load_rows(layer, U_PLE, ple_proj, 0)
                for n in range(4):
                    load_rows(layer, U_PLE + 1 + n, ple_gate_w, n)
            sp.wait_ge(x_done, DEPTH)
            sp.dma_start(out[0].rearrange("(t p) d -> p t d", p=P), x[:, :, :]).then_inc(stored, 16)
            sp.wait_ge(stored, 16)

        @block.gpsimd
        def _(pool):
            made = [0]

            def link(instruction):
                instruction.then_inc(consts_ready, 1)
                made[0] += 1

            def settle():
                pool.wait_ge(consts_ready, made[0])

            for tile, value in ((ident, 0.0), (ones, 1.0), (neg_ones, -1.0), (neg_later, -1.0),
                                (causal, 1.0), (head_mean, 0.0), (eps_col, EPS), (param_rows, 0.0)):
                link(nc.gpsimd.memset(tile[:, :], value))
            for tile in (xpad, xc_pad, bd_a, bd_x, bd_p, sums[0], sums[1], sums[2], sums[3]):
                link(nc.gpsimd.memset(tile[:, :, :], 0.0))
            link(nc.gpsimd.iota(count_i[:, :, :], pattern=[[0, 2], [1, SEQ]], base=1, channel_multiplier=0))
            settle()
            link(nc.gpsimd.tensor_copy(inv_count[:, :, :], count_i[:, :, :]))
            link(nc.gpsimd.affine_select(out=ident[:, :], in_=ident[:, :], compare_op=ALU.not_equal, fill=1.0,
                                         base=0, pattern=[[-1, P]], channel_multiplier=1))
            link(nc.gpsimd.affine_select(out=neg_later[:, :], in_=neg_later[:, :], compare_op=ALU.is_gt,
                                         fill=0.0, base=0, pattern=[[-1, P]], channel_multiplier=1))
            link(nc.gpsimd.affine_select(out=causal[:, :], in_=causal[:, :], compare_op=ALU.is_gt,
                                         fill=0.0, base=0, pattern=[[1, P]], channel_multiplier=-1))
            for b in range(P // DH):
                settle()
                blk = slice(b * DH, (b + 1) * DH)
                link(nc.gpsimd.memset(head_mean[blk, blk], 1.0 / DH))
            for n, w in enumerate(WINDOWS):
                settle()
                blk = slice((n % 2) * DH, (n % 2 + 1) * DH)
                link(nc.gpsimd.tensor_scalar(inv_count[blk, n // 2, :], inv_count[blk, n // 2, :],
                                             float(w), None, ALU.min))

            assert made[0] == CONSTS

            with pool.Fori(0, DEPTH) as layer:
                def mask_w(h):
                    pool.wait_ge(w_exped, layer * HEADS + h + 1)
                    diagonal = logs[h % HB][:, :].rearrange("p (b c) -> p b c", b=3)[:, 0:3:2, :]
                    nc.gpsimd.tensor_tensor(diagonal, diagonal,
                                            causal[:, :].unsqueeze(1).to_broadcast([P, 2, P]),
                                            ALU.mult).then_inc(w_ready, 1)

                pool.wait_ge(inverse_ready, 1)
                step = Steps(pool, pool_step, 8)
                step.start_layer(layer)
                for h in range(HEADS):
                    mask_w(h)
                pool.wait_ge(evacuated, layer * 4 + 4)
                source, width = xc_pad, 1
                for n, total in enumerate(sums):
                    chunks = slice(0, 2) if n < 2 else slice(1, 2)
                    here = slice(0, 2) if n < 2 else slice(0, 1)
                    src = source[:, chunks, :] if n <= 2 else source[:, 0:1, :]
                    lo = 2 * width - 1 if n < 3 else PADW
                    step.done(nc.gpsimd.tensor_tensor(total[:, here, lo:], src[:, :, lo:],
                                                      src[:, :, lo - width:PADW + SEQ - width], ALU.add))
                    step.settle()
                    source, width = total, 2 * width
                for n, total in enumerate(sums):
                    blk = slice((n % 2) * DH, (n % 2 + 1) * DH)
                    step.done(nc.gpsimd.tensor_tensor(pooled[blk, n // 2, :], total[blk, 0, PADW:],
                                                      inv_count[blk, n // 2, :], ALU.mult))
                    step.settle()
                nc.gpsimd.tensor_tensor(pooled[:, :, :], pooled[:, :, :], xc_pad[:, :, PADW:],
                                        ALU.subtract).then_inc(pooled_ready, 1)
                step.end_layer()

        @block.scalar
        def _(act):
            act.wait_ge(consts_ready, CONSTS)
            with act.Fori(0, DEPTH) as layer:
                step = Steps(act, act_step, ACT_STEPS)
                step.start_layer(layer)

                def split(offset, width=UNIT, j=0):
                    slot = offset % RING
                    act.wait_ge(slot_loaded[slot], 16 * HALVES * slot_use(layer, offset, j))
                    act.wait_ge(unit_used, unit_count(layer, offset, j))
                    nc.scalar.activation(whi[slot][:, 0:width], raw[slot][:, 0:width], ACT.Copy
                                         ).then_inc(hi_split, 1)

                def norm(i):
                    for q in range(4):
                        t, h = q // 2, q % 2
                        act.wait_ge(xt_turned, layer * 16 + 4 * i + q + 1)
                        nc.scalar.activation(xt_hi[:, 4 * h:4 * h + 4, t * P:(t + 1) * P],
                                             acc[q][:, :].rearrange("p (k n) -> p k n", k=4),
                                             ACT.Copy).then_inc(xt_rounded, 1)
                    for q in range(4):
                        t, h = q // 2, q % 2
                        last = nc.scalar.activation(scratch[:, q, :], x[:, t, h * BANK:(h + 1) * BANK],
                                                    ACT.Square, accum_out=square_sums[:, q:q + 1])
                    last.then_inc(squares_summed, 1)
                    act.wait_ge(mean_ready, layer * 4 + i + 1)
                    nc.scalar.activation(rms[:, :], mean_sq[:, :], ACT.Sqrt, bias=eps_col[:, :],
                                         scale=1.0 / D).then_inc(rms_ready, 1)

                def ffn(f, i, base):
                    def silus(j):
                        for t in range(T):
                            up_product_ready(act, layer, f, base, j, t)
                            nc.scalar.activation(silu[:, t, :], up[t][:, 0:GROUP], ACT.Silu,
                                                 scale=rstd[:, t:t + 1]).then_inc(silu_ready, 1)

                    def round_gt(j):
                        act.wait_ge(g_turned, layer * 2 * GROUPS + f * GROUPS + j + 1)
                        nc.scalar.activation(gt_hi[:, :, :, :],
                                             turn[0][:, :].rearrange("p (c t n) -> p c t n", c=2, t=T),
                                             ACT.Copy).then_inc(gt_rounded, 1)

                    split(base + 2)
                    act.wait_ge(rstd_ready, layer * 4 + i + 1)
                    silus(0)
                    split(base + 3)
                    round_gt(0)
                    with act.Fori(1, GROUPS) as j:
                        split(base + 1, j=j)
                        split(base + 2, j=j)
                        act.wait_ge(gated_ready, layer * 4 * GROUPS + (f * GROUPS + j) * 2)
                        silus(j)
                        split(base + 3, j=j)
                        round_gt(j)

                def params():
                    act.wait_ge(params_turned, layer + 1)
                    step.done(nc.scalar.activation(par[:, :], turn[1][:, 0:ROWS], ACT.Copy))
                    step.settle()
                    step.done(nc.scalar.activation(tiny[:, 0, :], par[:, ROW_LAM:ROW_LAM + LC], ACT.Abs))
                    step.settle()
                    nc.scalar.activation(tiny[:, 1, :], tiny[:, 0, :], ACT.Exp, scale=-1.0
                                         ).then_inc(lam_exp_ready, 1)

                split(U_FFN1)
                split(U_FFN1 + 1)
                norm(0)
                ffn(0, 0, U_FFN1)
                split(U_MIX + 1)
                params()

                norm(1)
                split(U_MIX + 2)
                act.wait_ge(rrow_turned, layer + 1)
                nc.scalar.activation(rrow[:, :], turn[1][:, 0:SEQ], ACT.Copy).then_inc(rrow_ready, 1)
                for g in range(3):
                    act.wait_ge(qk_scaled, layer * 3 + g + 1)
                    nc.scalar.activation(qk_sq[:, 2 * g:2 * g + 2, :], qk[:, 2 * g:2 * g + 2, :],
                                         ACT.Square).then_inc(qk_squared, 1)
                    if g < 2:
                        split(U_MIX + 3 + g, 4 * D_SB)
                for g, bank in enumerate((turn[0], turn[1], acc[3])):
                    act.wait_ge(qk_summed, layer * 3 + g + 1)
                    step.done(nc.scalar.activation(qk_sq[:, 2 * g:2 * g + 2, :],
                                                   bank[:, :].rearrange("p (c n) -> p c n", c=2),
                                                   ACT.Ln, bias=eps_col[:, :]))
                step.settle()
                for g in range(3):
                    nc.scalar.activation(qk_sq[:, 2 * g:2 * g + 2, :], qk_sq[:, 2 * g:2 * g + 2, :],
                                         ACT.Exp, scale=-0.5).then_inc(qk_rstd, 1)
                split(U_MIX + 5)
                split(U_MIX + 6)
                for t in range(T):
                    wait_unit(act, layer, U_MIX + 4)
                    nc.scalar.activation(v[:, t, :], up[t][:, 0:D_SB], ACT.Copy, scale=rstd[:, t:t + 1]
                                         ).then_inc(v_ready, 1)

                def head_logs(first):
                    for h in range(first, first + HB):
                        act.wait_ge(z_ready, layer * HEADS + h + 1)
                        if h >= HB:
                            act.wait_ge(o_ready, layer * HEADS + h - HB + 1)
                        step.done(nc.scalar.activation(logs[h % HB][:, :], head_bank[h % HB][:, 0:3 * P], ACT.Abs))
                    step.settle()
                    for h in range(first, first + HB):
                        step.done(nc.scalar.activation(logs[h % HB][:, :], logs[h % HB][:, :], ACT.Exp, scale=-1.0))
                    step.settle()
                    for h in range(first, first + HB):
                        nc.scalar.activation(logs[h % HB][:, :], logs[h % HB][:, :], ACT.Ln, bias=ones[:, 0:1]
                                             ).then_inc(log_ready, 1)

                def head_weights(first):
                    for h in range(first, first + HB):
                        act.wait_ge(logw_ready, layer * HEADS + h + 1)
                        nc.scalar.activation(logs[h % HB][:, :], lbeta[h % HB][:, :], ACT.Exp
                                             ).then_inc(w_exped, 1)

                def round_o(c):
                    act.wait_ge(o_ready, layer * HEADS + 2 * c + 2)
                    nc.scalar.activation(mix_hi[:, c, :], turn[0][:, 0:SEQ], ACT.Copy).then_inc(o_rounded, 1)

                head_logs(0)
                split(U_MIX + 7)
                head_weights(0)
                split(U_MIX + 8)
                round_o(0)
                head_logs(3)
                split(U_MIX + 9)
                head_weights(3)
                split(U_MIX + 10)
                round_o(1)
                round_o(2)
                act.wait_ge(pool_product, layer + 1)
                for c in range(2):
                    last = nc.scalar.activation(mix_hi[:, KC - 2 + c, :], acc[3][:, c * SEQ:(c + 1) * SEQ],
                                                ACT.Copy, scale=par[:, ROW_SCALE + c:ROW_SCALE + c + 1])
                last.then_inc(pool_rounded, 1)
                for c in range(LC):
                    act.wait_ge(gates_product, layer * LC + c + 1)
                    nc.scalar.activation(r_gate[:, c, :], acc[c][:, 0:SEQ], ACT.Sigmoid,
                                         bias=par[:, ROW_BA + c:ROW_BA + c + 1])
                    step.done(nc.scalar.activation(i_gate[:, c, :], acc[c][:, SEQ:2 * SEQ], ACT.Sigmoid,
                                                   bias=par[:, ROW_BX + c:ROW_BX + c + 1]))
                step.settle()
                act.wait_ge(decay_ready, layer + 1)
                for c in range(LC):
                    last = nc.scalar.activation(th[:, c, :], r_gate[:, c, :], ACT.Tanh,
                                                scale=decay_scale[:, c:c + 1])
                last.then_inc(tanh_ready, 1)
                act.wait_ge(tanh_ready, layer + 1)
                nc.scalar.activation(r_gate[:, :, :], th[:, :, :], ACT.Sqrt, scale=-4.0).then_inc(root_ready, 1)
                nc.scalar.activation(gb[:, :, :], gb[:, :, :], ACT.Gelu_apprx_tanh).then_inc(gelu_ready, 1)
                split(U_MIX + 11)
                split(U_MIX + 12)
                act.wait_ge(lru_ready, layer + 1)
                nc.scalar.activation(mix_hi[:, 3:6, :], gb[:, :, :], ACT.Copy).then_inc(lru_rounded, 1)
                split(U_FFN2)
                split(U_FFN2 + 1)

                norm(2)
                ffn(1, 2, U_FFN2)
                act.wait_ge(p_turned, layer + 1)
                nc.scalar.activation(pt_hi[:, :, :], turn[1][:, :].rearrange("p (c n) -> p c n", c=2),
                                     ACT.Copy).then_inc(p_rounded, 1)
                split(U_PLE + 1)

                split(U_PLE + 2)
                norm(3)
                split(U_PLE + 3)
                split(U_PLE + 4)
                act.wait_ge(rstd_ready, layer * 4 + 4)
                for q in range(4):
                    t = q // 2
                    wait_quarter(act, layer, 3, q, UNITS - 1)
                    nc.scalar.activation(scratch[:, q, :], acc[q][:, :], ACT.Sigmoid,
                                         scale=rstd[:, t:t + 1]).then_inc(sig_ready, 1)
                step.end_layer()

        @block.vector
        def _(dve):
            nc.vector.memset(square_sums[:, 0:1], 0.0).then_inc(lo_split, RING)
            nc.vector.memset(square_sums[:, 1:2], 0.0).then_inc(unit_used, RING)
            dve.wait_ge(consts_ready, CONSTS)
            nc.vector.reciprocal(inv_count[:, :, :], inv_count[:, :, :]).then_inc(inverse_ready, 1)
            dve.wait_ge(x_loaded, 16)
            with dve.Fori(0, DEPTH) as layer:
                step = Steps(dve, dve_step, DVE_STEPS)
                step.start_layer(layer)

                def split(offset, width=UNIT, j=0):
                    slot = offset % RING
                    dve.wait_ge(hi_split, unit_count(layer, offset, j))
                    nc.vector.tensor_tensor(wlo[slot][:, 0:width], raw[slot][:, 0:width],
                                            whi[slot][:, 0:width].bitcast(F32), ALU.subtract
                                            ).then_inc(lo_split, 1)

                def quarter(tile, q):
                    return tile[:, q // 2, (q % 2) * BANK:(q % 2 + 1) * BANK]

                def apply_gain(i, q):
                    nc.vector.tensor_tensor(quarter(xg, q), quarter(x, q),
                                            gain[i % 2][:, (q % 2) * BANK:(q % 2 + 1) * BANK],
                                            ALU.mult).then_inc(gained, 1)

                def residual(i, scale):
                    dve.wait_ge(gain_loaded[i % 2], 16 * (layer * 2 + i // 2 + 1))
                    for q in range(4):
                        wait_quarter(dve, layer, i - 1, q, PHASE_ENDS[i - 1])
                        step.done(nc.vector.scalar_tensor_tensor(
                            out=quarter(x, q), in0=acc[q][:, :], scalar=scale, in1=quarter(x, q),
                            op0=ALU.mult, op1=ALU.add))
                        step.settle()
                        apply_gain(i, q)

                def norm(i):
                    for q in range(4):
                        t, h = q // 2, q % 2
                        dve.wait_ge(xt_rounded, layer * 16 + 4 * i + q + 1)
                        cols = (slice(None), slice(4 * h, 4 * h + 4), slice(t * P, (t + 1) * P))
                        nc.vector.tensor_tensor(xt_lo[cols], acc[q][:, :].rearrange("p (k n) -> p k n", k=4),
                                                xt_hi[cols].bitcast(F32), ALU.subtract).then_inc(xt_split, 1)
                    dve.wait_ge(squares_summed, layer * 4 + i + 1)
                    nc.vector.tensor_tensor(mean_sq[:, :], square_sums[:, 0:4:2], square_sums[:, 1:4:2],
                                            ALU.add).then_inc(mean_ready, 1)
                    dve.wait_ge(rms_ready, layer * 4 + i + 1)
                    nc.vector.reciprocal(rstd[:, :], rms[:, :]).then_inc(rstd_ready, 1)

                def ffn(f, i, base):
                    def gates(j):
                        for t in range(T):
                            dve.wait_ge(silu_ready, layer * 4 * GROUPS + (f * GROUPS + j) * 2 + t + 1)
                            nc.vector.scalar_tensor_tensor(
                                out=gated[:, t, :], in0=up[t][:, GROUP:2 * GROUP], scalar=rstd[:, t:t + 1],
                                in1=silu[:, t, :], op0=ALU.mult, op1=ALU.mult).then_inc(gated_ready, 1)

                    def split_gt(j):
                        dve.wait_ge(gt_rounded, layer * 2 * GROUPS + f * GROUPS + j + 1)
                        nc.vector.tensor_tensor(gt_lo[:, :, :, :].rearrange("p c t n -> p (c t n)"), turn[0][:, :],
                                                gt_hi[:, :, :, :].bitcast(F32).rearrange("p c t n -> p (c t n)"),
                                                ALU.subtract).then_inc(gt_split, 1)

                    split(base + 2)
                    dve.wait_ge(rstd_ready, layer * 4 + i + 1)
                    gates(0)
                    split(base + 3)
                    split_gt(0)
                    with dve.Fori(1, GROUPS) as j:
                        split(base + 1, j=j)
                        split(base + 2, j=j)
                        gates(j)
                        split(base + 3, j=j)
                        split_gt(j)

                def params():
                    dve.wait_ge(lam_exp_ready, layer + 1)
                    e, den, s, s2, poly = (tiny[:, n, :] for n in (1, 2, 3, 4, 5))
                    lam = par[:, ROW_LAM:ROW_LAM + LC]

                    def link(instruction):
                        step.done(instruction)
                        step.settle()

                    link(nc.vector.tensor_scalar(den, e, 2.0, None, ALU.add))
                    link(nc.vector.reciprocal(den, den))
                    link(nc.vector.tensor_tensor(s, e, den, ALU.mult))
                    link(nc.vector.tensor_tensor(s2, s, s, ALU.mult))
                    link(nc.vector.tensor_scalar(poly, s2, 1.0 / 15, None, ALU.mult))
                    for odd in (13, 11, 9, 7, 5, 3):
                        link(nc.vector.scalar_tensor_tensor(out=poly, in0=poly, scalar=1.0 / odd, in1=s2,
                                                            op0=ALU.add, op1=ALU.mult))
                    link(nc.vector.scalar_tensor_tensor(out=poly, in0=poly, scalar=1.0, in1=s,
                                                        op0=ALU.add, op1=ALU.mult))
                    link(nc.vector.tensor_scalar(s, lam, 0.0, 4.0, ALU.min, ALU.mult))
                    nc.vector.scalar_tensor_tensor(out=decay_scale[:, :], in0=poly, scalar=-8.0, in1=s,
                                                   op0=ALU.mult, op1=ALU.add).then_inc(decay_ready, 1)
                    link(nc.vector.scalar_tensor_tensor(
                        out=qk_gain[:, :], in0=par[:, ROW_QN:ROW_QN + 1], scalar=float(DH) ** -0.5,
                        in1=par[:, ROW_KN:ROW_KN + 1], op0=ALU.mult, op1=ALU.mult))

                dve.wait_ge(gain_loaded[0], 16 * (layer * 2 + 1))
                for q in range(4):
                    apply_gain(0, q)
                split(U_FFN1)
                split(U_FFN1 + 1)
                norm(0)
                ffn(0, 0, U_FFN1)
                split(U_MIX + 1)
                params()

                residual(1, 0.5)
                norm(1)
                split(U_MIX + 2)
                dve.wait_ge(rstd_ready, layer * 4 + 2)
                for t in range(T):
                    last = nc.vector.tensor_scalar(diag[:, t * P:(t + 1) * P], ident[:, :], rstd[:, t:t + 1],
                                                   None, ALU.mult)
                last.then_inc(diag_ready, 1)
                rr = rrow[:, :].unsqueeze(1).to_broadcast([P, 2, SEQ])

                def chunks(bank, n=2):
                    return bank[:, :].rearrange("p (c n) -> p c n", c=2)

                dve.wait_ge(rrow_ready, layer + 1)
                for g in range(3):
                    wait_unit(dve, layer, U_MIX + g)
                    nc.vector.tensor_tensor(qk[:, 2 * g:2 * g + 2, :], chunks(acc[g]), rr, ALU.mult
                                            ).then_inc(qk_scaled, 1)
                    if g < 2:
                        split(U_MIX + 3 + g, 4 * D_SB)
                for g in range(3):
                    dve.wait_ge(qk_rstd, layer * 3 + g + 1)
                    last = nc.vector.tensor_tensor(qk[:, 2 * g:2 * g + 2, :], qk[:, 2 * g:2 * g + 2, :],
                                                   qk_sq[:, 2 * g:2 * g + 2, :], ALU.mult)
                step.done(last)
                step.settle()
                nc.vector.tensor_scalar(qk[:, 0:3, :], qk[:, 0:3, :], qk_gain[:, :], None, ALU.mult
                                        ).then_inc(qk_normed, 1)
                split(U_MIX + 5)
                split(U_MIX + 6)

                def head_keeps(first):
                    for h in range(first, first + HB):
                        b = h % HB
                        bank = head_bank[b][:, 0:3 * P]
                        dve.wait_ge(log_ready, layer * HEADS + h + 1)
                        step.done(nc.vector.scalar_tensor_tensor(out=soft[b][:, :], in0=bank, scalar=0.0,
                                                                 in1=logs[b][:, :], op0=ALU.max, op1=ALU.add))
                        step.done(nc.vector.scalar_tensor_tensor(out=lbeta[b][:, :], in0=bank, scalar=0.0,
                                                                 in1=logs[b][:, :], op0=ALU.min, op1=ALU.subtract))
                        step.settle()
                        diagonal = soft[b][:, :].rearrange("p (b c) -> p b c", b=3)[:, 0:3:2, :]
                        nc.vector.tensor_tensor(diagonal, diagonal,
                                                causal[:, :].unsqueeze(1).to_broadcast([P, 2, P]),
                                                ALU.mult).then_inc(keep_ready, 1)

                def head_sums(first):
                    for h in range(first, first + HB):
                        b = h % HB
                        dve.wait_ge(suffix_ready, layer * HEADS + h + 1)
                        nc.vector.tensor_tensor(lbeta[b][:, :], head_bank[b][:, 0:3 * P], lbeta[b][:, :],
                                                ALU.add).then_inc(logw_ready, 1)

                def split_o(c):
                    dve.wait_ge(o_rounded, layer * 3 + c + 1)
                    nc.vector.tensor_tensor(mix_lo[:, c, :], turn[0][:, 0:SEQ], mix_hi[:, c, :].bitcast(F32),
                                            ALU.subtract).then_inc(att_split, 1)

                def evacuate(n, parts):
                    wait_unit(dve, layer, U_MIX + 5 + n)
                    for dst, src, row in parts:
                        last = nc.vector.tensor_tensor(dst, src, row, ALU.mult)
                    last.then_inc(evacuated, 1)

                head_keeps(0)
                split(U_MIX + 7)
                evacuate(0, [(xpad[:, 0:2, TAPS - 1:], chunks(acc[0]), rr)])
                head_sums(0)
                split(U_MIX + 8)
                evacuate(1, [(xpad[:, 2, TAPS - 1:], acc[1][:, 0:SEQ], rrow[:, :]),
                             (gb[:, 0, :], acc[1][:, SEQ:2 * SEQ], rrow[:, :])])
                split_o(0)
                dve.wait_ge(evacuated, layer * 4 + 2)
                for w in range(TAPS):
                    for c in range(LC):
                        cw = par[:, ROW_CONV_W + w * LC + c:ROW_CONV_W + w * LC + c + 1]
                        window = xpad[:, c, w:w + SEQ]
                        if w == 0:
                            last = nc.vector.tensor_scalar(xconv[:, c, :], window, cw,
                                                           par[:, ROW_CONV_B + c:ROW_CONV_B + c + 1],
                                                           ALU.mult, ALU.add)
                        else:
                            last = nc.vector.scalar_tensor_tensor(out=xconv[:, c, :], in0=window, scalar=cw,
                                                                  in1=xconv[:, c, :], op0=ALU.mult, op1=ALU.add)
                        if w < TAPS - 1:
                            step.done(last)
                    if w < TAPS - 1:
                        step.settle()
                last.then_inc(conv_ready, 1)
                head_keeps(3)
                split(U_MIX + 9)
                evacuate(2, [(gb[:, 1:3, :], chunks(acc[2]), rr)])
                head_sums(3)
                split(U_MIX + 10)
                evacuate(3, [(xc_pad[:, :, PADW:], chunks(acc[3]), rr)])
                split_o(1)
                split_o(2)
                dve.wait_ge(pool_rounded, layer + 1)
                for c in range(2):
                    last = nc.vector.scalar_tensor_tensor(
                        out=mix_lo[:, KC - 2 + c, :], in0=acc[3][:, c * SEQ:(c + 1) * SEQ],
                        scalar=par[:, ROW_SCALE + c:ROW_SCALE + c + 1], in1=mix_hi[:, KC - 2 + c, :].bitcast(F32),
                        op0=ALU.mult, op1=ALU.subtract)
                last.then_inc(pool_split, 1)
                dve.wait_ge(tanh_ready, layer + 1)
                step.done(nc.vector.tensor_scalar(rec[:, :, :], th[:, :, :], -1.0, 1.0, ALU.mult, ALU.add))
                step.settle()
                step.done(nc.vector.reciprocal(rec[:, :, :], rec[:, :, :]))
                step.done(nc.vector.tensor_tensor(i_gate[:, :, :], i_gate[:, :, :], xconv[:, :, :], ALU.mult))
                step.settle()
                step.done(nc.vector.scalar_tensor_tensor(out=decay[:, :, :], in0=th[:, :, :], scalar=1.0,
                                                         in1=rec[:, :, :], op0=ALU.add, op1=ALU.mult))
                dve.wait_ge(root_ready, layer + 1)
                step.done(nc.vector.tensor_tensor(rec[:, :, :], rec[:, :, :], r_gate[:, :, :], ALU.mult))
                step.settle()
                step.done(nc.vector.tensor_tensor(rec[:, :, :], rec[:, :, :], i_gate[:, :, :], ALU.mult))
                step.settle()
                for c in range(LC):
                    last = nc.vector.tensor_tensor_scan(th[:, c, :], decay[:, c, :], rec[:, c, :], 0.0,
                                                        ALU.mult, ALU.add)
                step.done(last)
                step.settle()
                dve.wait_ge(gelu_ready, layer + 1)
                nc.vector.tensor_tensor(gb[:, :, :], gb[:, :, :], th[:, :, :], ALU.mult).then_inc(lru_ready, 1)
                split(U_MIX + 11)
                split(U_MIX + 12)
                dve.wait_ge(lru_rounded, layer + 1)
                nc.vector.tensor_tensor(mix_lo[:, 3:6, :], gb[:, :, :], mix_hi[:, 3:6, :].bitcast(F32),
                                        ALU.subtract).then_inc(lru_split, 1)
                split(U_FFN2)
                split(U_FFN2 + 1)

                residual(2, 1.0)
                norm(2)
                ffn(1, 2, U_FFN2)
                dve.wait_ge(p_rounded, layer + 1)
                nc.vector.tensor_tensor(pt_lo[:, :, :], chunks(turn[1]), pt_hi[:, :, :].bitcast(F32),
                                        ALU.subtract).then_inc(p_split, 1)
                split(U_PLE + 1)

                residual(3, 0.5)
                split(U_PLE + 2)
                norm(3)
                split(U_PLE + 3)
                split(U_PLE + 4)
                for q in range(4):
                    dve.wait_ge(sig_ready, layer * 4 + q + 1)
                    step.done(nc.vector.tensor_tensor(scratch[:, q, :], proj_bank[q][:, :], scratch[:, q, :],
                                                      ALU.mult))
                    step.settle()
                    last = nc.vector.tensor_tensor(quarter(x, q), quarter(x, q), scratch[:, q, :], ALU.add)
                last.then_inc(x_done, 1)
                dve.wait_ge(x_done, layer + 1)
                step.end_layer()

        @block.tensor
        def _(pe):
            pe.wait_ge(consts_ready, CONSTS)
            with pe.Fori(0, DEPTH) as layer:
                def unit_split(offset, j=0):
                    pe.wait_ge(lo_split, unit_count(layer, offset, j) + RING)

                def three(bank, a_hi, a_lo, b_hi, b_lo, start, stop):
                    nc.tensor.matmul(bank, a_hi, b_hi, start=start, stop=False)
                    nc.tensor.matmul(bank, a_hi, b_lo, start=False, stop=False)
                    return nc.tensor.matmul(bank, a_lo, b_hi, start=False, stop=stop)

                def turn_x(i):
                    for q in range(4):
                        t, h = q // 2, q % 2
                        pe.wait_ge(gained, layer * 16 + 4 * i + q + 1)
                        for k in range(4):
                            last = nc.tensor.transpose(acc[q][:, k * P:(k + 1) * P],
                                                       xg[:, t, (4 * h + k) * P:(4 * h + k + 1) * P],
                                                       ident[:, :])
                        last.then_inc(xt_turned, 1)

                def rows_unit(offset, a_hi, a_lo, chunks, banks, first, phase_end=False, j=0, stop=False):
                    slot = offset % RING
                    unit_split(offset, j)
                    for c in range(2):
                        for t in range(T):
                            for h in range(2):
                                cols = slice(c * D + h * BANK, c * D + (h + 1) * BANK)
                                last = three(banks[2 * t + h][:, :], a_hi(chunks[c], t), a_lo(chunks[c], t),
                                             whi[slot][:, cols], wlo[slot][:, cols],
                                             start=first and c == 0, stop=(phase_end or stop) and c == 1)
                                if phase_end and c == 1 and 2 * t + h < 3:
                                    last.then_inc(acc_ready, 1)
                    last.then_inc(unit_used, 1)

                def of(tile):
                    return lambda k, t: tile[:, k, t * P:(t + 1) * P]

                def ffn(f, base, before_last):
                    def up_group(offset, j):
                        for half in range(2):
                            o = offset + half
                            slot = o % RING
                            unit_split(o, j)
                            for t in range(T):
                                for kk in range(4):
                                    k = 4 * half + kk
                                    cols = slice(kk * BANK, (kk + 1) * BANK)
                                    last = three(up[t][:, :], of(xt_hi)(k, t), of(xt_lo)(k, t),
                                                 whi[slot][:, cols], wlo[slot][:, cols],
                                                 start=k == 0, stop=k == KC - 1)
                                if half == 1 and t == 0:
                                    last.then_inc(up_ready, 1)
                            last.then_inc(unit_used, 1)

                    def turn_g(g):
                        pe.wait_ge(gated_ready, layer * 4 * GROUPS + (f * GROUPS + g) * 2 + 2)
                        for c in range(2):
                            for t in range(T):
                                last = nc.tensor.transpose(turn[0][:, (c * T + t) * P:(c * T + t + 1) * P],
                                                           gated[:, t, c * P:(c + 1) * P], ident[:, :])
                        last.then_inc(g_turned, 1)

                    def down(offset, j, g, first, phase_end=False):
                        pe.wait_ge(gt_split, layer * 2 * GROUPS + f * GROUPS + g + 1)
                        rows_unit(offset, lambda c, t: gt_hi[:, c, t, :], lambda c, t: gt_lo[:, c, t, :],
                                  (0, 1), acc, first, phase_end, j)

                    up_group(base, 0)
                    turn_g(0)
                    up_group(base - 1, 1)
                    down(base + 1, 1, 0, True)
                    turn_g(1)
                    with pe.Fori(2, GROUPS) as j:
                        up_group(base - 1, j)
                        down(base + 1, j, j - 1, False)
                        turn_g(j)
                    before_last()
                    down(base - 1, GROUPS, GROUPS - 1, False, True)

                def turn_params():
                    pe.wait_ge(params_loaded, 16 * PARAM_DMAS * (layer + 1))
                    nc.tensor.transpose(turn[1][:, 0:P], param_rows[:, :], ident[:, :]
                                        ).then_inc(params_turned, 1)

                def turn_p():
                    pe.wait_ge(p_loaded, 16 * (layer + 1))
                    for c in range(2):
                        for t in range(T):
                            last = nc.tensor.transpose(turn[1][:, (c * T + t) * P:(c * T + t + 1) * P],
                                                       pl[:, t, c * P:(c + 1) * P], ident[:, :])
                    last.then_inc(p_turned, 1)

                def xt_wait(i):
                    pe.wait_ge(xt_split, layer * 16 + 4 * i + 4)

                turn_x(0)
                xt_wait(0)
                ffn(0, U_FFN1, turn_params)

                turn_x(1)
                xt_wait(1)

                def features(n, bank):
                    slot = (U_MIX + n) % RING
                    unit_split(U_MIX + n)
                    for c in range(2):
                        out_ = bank[:, c * SEQ:(c + 1) * SEQ]
                        for k in range(KC):
                            cols = slice(k * 256 + c * P, k * 256 + (c + 1) * P)
                            nc.tensor.matmul(out_, whi[slot][:, cols], xt_hi[:, k, :], start=k == 0, stop=False)
                            nc.tensor.matmul(out_, whi[slot][:, cols], xt_lo[:, k, :], start=False, stop=False)
                            last = nc.tensor.matmul(out_, wlo[slot][:, cols], xt_hi[:, k, :], start=False,
                                                    stop=k == KC - 1)
                    last.then_inc(unit_used, 1)

                def head_z(h):
                    if h == 0:
                        pe.wait_ge(qk_normed, layer + 1)
                        pe.wait_ge(v_ready, layer * T + T)
                    if h >= HB:
                        pe.wait_ge(logw_ready, layer * HEADS + h - HB + 1)
                    rows, c, bank = slice(h % 2 * DH, (h % 2 + 1) * DH), h // 2, head_bank[h % HB]
                    nc.tensor.matmul(bank[:, 0:2 * P], qk[rows, 3 + c, 0:P], qk[rows, c, :], start=True, stop=True)
                    nc.tensor.matmul(bank[:, 2 * P:3 * P], qk[rows, 3 + c, P:2 * P], qk[rows, c, P:2 * P],
                                     start=True, stop=True).then_inc(z_ready, 1)

                def head_suffix(h):
                    pe.wait_ge(keep_ready, layer * HEADS + h + 1)
                    bank = head_bank[h % HB]
                    nc.tensor.matmul(bank[:, 0:3 * P], neg_later[:, :], soft[h % HB][:, :], start=True, stop=False)
                    nc.tensor.matmul(bank[:, P:2 * P], neg_ones[:, :], soft[h % HB][:, 2 * P:3 * P],
                                     start=False, stop=True).then_inc(suffix_ready, 1)

                def head_out(h):
                    pe.wait_ge(w_ready, layer * HEADS + h + 1)
                    if h % 2 == 0 and h >= 2:
                        pe.wait_ge(att_split, layer * 3 + h // 2)
                    rows, cols = slice(h % 2 * DH, (h % 2 + 1) * DH), slice(h * DH, (h + 1) * DH)
                    nc.tensor.matmul(turn[0][rows, 0:2 * P], v[:, 0, cols], logs[h % HB][:, 0:2 * P],
                                     start=True, stop=False)
                    nc.tensor.matmul(turn[0][rows, P:2 * P], v[:, 1, cols], logs[h % HB][:, 2 * P:3 * P],
                                     start=False, stop=True).then_inc(o_ready, 1)

                features(0, acc[0])
                pe.wait_ge(diag_ready, layer + 1)
                nc.tensor.matmul(turn[1][:, 0:SEQ], ones[:, :], diag[:, :], start=True, stop=True
                                 ).then_inc(rrow_turned, 1)
                features(1, acc[1])
                features(2, acc[2])
                for g, bank in enumerate((turn[0], turn[1], acc[3])):
                    pe.wait_ge(qk_squared, layer * 3 + g + 1)
                    nc.tensor.matmul(bank[:, :], head_mean[:, :], qk_sq[:, 2 * g:2 * g + 2, :],
                                     start=True, stop=True).then_inc(qk_summed, 1)
                for half in range(2):
                    slot = (U_MIX + 3 + half) % RING
                    unit_split(U_MIX + 3 + half)
                    for t in range(T):
                        for kk in range(4):
                            k = 4 * half + kk
                            cols = slice(kk * D_SB, (kk + 1) * D_SB)
                            last = three(up[t][:, 0:D_SB], of(xt_hi)(k, t), of(xt_lo)(k, t),
                                         whi[slot][:, cols], wlo[slot][:, cols], start=k == 0, stop=k == KC - 1)
                    last.then_inc(unit_used, 1)
                for h in range(0, 3):
                    head_z(h)
                features(5, acc[0])
                for h in range(0, 3):
                    head_suffix(h)
                features(6, acc[1])
                for h in range(0, 3):
                    head_out(h)
                for h in range(3, 6):
                    head_z(h)
                features(7, acc[2])
                for h in range(3, 6):
                    head_suffix(h)
                features(8, acc[3])
                head_out(3)
                pe.wait_ge(conv_ready, layer + 1)
                pe.wait_ge(evacuated, layer * 4 + 3)
                for c in range(LC):
                    nc.tensor.matmul(acc[c][:, 0:SEQ], bd_a[:, c, :], xconv[:, c, :], start=True, stop=True)
                    nc.tensor.matmul(acc[c][:, SEQ:2 * SEQ], bd_x[:, c, :], xconv[:, c, :], start=True, stop=True
                                     ).then_inc(gates_product, 1)
                head_out(4)
                head_out(5)
                pe.wait_ge(pooled_ready, layer + 1)
                for c in range(2):
                    last = nc.tensor.matmul(acc[3][:, c * SEQ:(c + 1) * SEQ], bd_p[:, c, :], pooled[:, c, :],
                                            start=True, stop=True)
                last.then_inc(pool_product, 1)
                pe.wait_ge(tanh_ready, layer + 1)
                pe.wait_ge(pool_split, layer + 1)
                rows_unit(U_MIX + 9, of(mix_hi), of(mix_lo), (6, 7), acc, True)
                pe.wait_ge(att_split, layer * 3 + 3)
                rows_unit(U_MIX + 10, of(mix_hi), of(mix_lo), (0, 1), acc, False)
                pe.wait_ge(lru_split, layer + 1)
                rows_unit(U_MIX + 11, of(mix_hi), of(mix_lo), (2, 3), acc, False)
                rows_unit(U_MIX + 12, of(mix_hi), of(mix_lo), (4, 5), acc, False, True)

                turn_x(2)
                xt_wait(2)
                ffn(1, U_FFN2, turn_p)

                pe.wait_ge(p_split, layer + 1)
                rows_unit(U_PLE, of(pt_hi), of(pt_lo), (0, 1), proj_bank, True, stop=True)
                turn_x(3)
                xt_wait(3)
                for n in range(4):
                    rows_unit(U_PLE + 1 + n, of(xt_hi), of(xt_lo), (2 * n, 2 * n + 1), acc, n == 0, n == 3)


_INS = ['x', 'p', 'ffn1_norm', 'ffn1_w1', 'ffn1_w3', 'ffn1_w2', 'mix_norm', 'w_in', 'q_norm', 'k_norm',
        'conv_w', 'conv_b', 'lru_wa', 'lru_ba', 'lru_wx', 'lru_bx', 'lru_lambda', 'pool_w', 'pool_scale',
        'w_out', 'ffn2_norm', 'ffn2_w1', 'ffn2_w3', 'ffn2_w2', 'ple_norm', 'ple_gate_w', 'ple_proj']


def kernel(**inputs):
    import concourse.bacc as bacc
    from concourse.bass_utils import run_bass_kernel_spmd

    nc = bacc.Bacc("TRN2", target_bir_lowering=False, num_devices=1)
    arrays, args = {}, []
    for name in _INS:
        a = np.ascontiguousarray(inputs[name])
        arrays[f"in_{name}"] = a
        args.append(nc.dram_tensor(f"in_{name}", a.shape, mybir.dt.from_np(a.dtype), kind="ExternalInput").ap())
    shape = inputs['x'].shape
    args.append(nc.dram_tensor("out_x", shape, F32, kind="ExternalOutput").ap())
    trunk_kernel(nc, *args)
    r = run_bass_kernel_spmd(nc, [arrays], core_ids=[0])
    return r.results[0]["out_x"]
```

```python
from contextlib import ExitStack

import numpy as np

import concourse.bass as bass
from concourse import mybir

P = 128
F32 = mybir.dt.float32
F32R = mybir.dt.float32r
I32 = mybir.dt.int32
ALU = mybir.AluOpType
ACT = mybir.ActivationFunctionType

RING = 3
HALVES = 2
UNIT = 2048
EPS = 1e-6
BANK = 512
WINDOWS = (2, 4, 8, 16)
POOL_SPLITS = (4, 6, 9)


class Steps:

    def __init__(self, engine, semaphore, per_layer):
        self.engine, self.semaphore, self.per_layer = engine, semaphore, per_layer
        self.base, self.count = 0, 0

    def start_layer(self, layer):
        self.base, self.count = layer * self.per_layer, 0

    def done(self, instruction):
        instruction.then_inc(self.semaphore, 1)
        self.count += 1

    def settle(self):
        self.engine.wait_ge(self.semaphore, self.base + self.count)

    def end_layer(self):
        assert self.count == self.per_layer, (self.semaphore, self.count)


def trunk_kernel(nc, x_in, p_in, ffn1_norm, ffn1_w1, ffn1_w3, ffn1_w2, mix_norm, w_in, q_norm, k_norm,
                 conv_w, conv_b, lru_wa, lru_ba, lru_wx, lru_bx, lru_lambda, pool_w, pool_scale,
                 w_out, ffn2_norm, ffn2_w1, ffn2_w3, ffn2_w2, ple_norm, ple_gate_w, ple_proj, out):
    DEPTH, D, FF = ffn1_w1.shape
    SEQ = x_in.shape[1]
    T = SEQ // P
    KC = D // P
    DH = q_norm.shape[1]
    PLE = ple_proj.shape[1]
    TAPS, D_LRU = conv_w.shape[1:]
    D_POOL = pool_scale.shape[1]
    D_SB = D - D_POOL - D_LRU
    HEADS = D_SB // DH
    LC = D_LRU // P
    GROUP = 256
    GROUPS = FF // GROUP
    assert (SEQ, D, DH, PLE, D_SB, D_LRU, D_POOL, TAPS) == (256, 1024, 64, 256, 384, 384, 256, 4)
    assert FF % GROUP == 0 and T == 2

    FFN_UNITS = 3 * GROUPS
    U_FFN1 = 0
    U_MIX = U_FFN1 + FFN_UNITS
    V, QK, XGC, WO = (0, 4), 1, 5, 9
    XGC_COLS = (0, 1, 3, 2)
    WO_ROWS = (3, 0, 2, 1)
    MIX_UNITS = 13
    U_FFN2 = U_MIX + MIX_UNITS
    U_PLE = U_FFN2 + FFN_UNITS
    PLE_UNITS = 5
    UNITS = U_PLE + PLE_UNITS
    assert UNITS % RING == 0
    POOL_UNITS = tuple(U_MIX + n for n in POOL_SPLITS)
    DVE_UNITS = UNITS - len(POOL_UNITS)
    assert U_FFN2 - 1 not in POOL_UNITS
    USES = UNITS // RING

    ROW_CONV_W = 0
    ROW_CONV_B = ROW_CONV_W + TAPS * LC
    ROW_BA = ROW_CONV_B + LC
    ROW_BX = ROW_BA + LC
    ROW_LAM = ROW_BX + LC
    ROW_SCALE = ROW_LAM + LC
    ROW_QN = ROW_SCALE + D_POOL // P
    ROW_KN = ROW_QN + 1
    ROWS = ROW_KN + 1
    PARAM_DMAS = 10 + 6

    with ExitStack() as ctx:
        def sb(name, shape, dt=F32):
            return ctx.enter_context(nc.sbuf_tensor(name, shape, dt))

        def sem(name):
            return ctx.enter_context(nc.semaphore(name))

        raw = [sb(f"raw{s}", [P, UNIT]) for s in range(RING)]
        whi = [sb(f"w_hi{s}", [P, UNIT], F32R) for s in range(RING)]
        wlo = [sb(f"w_lo{s}", [P, UNIT], F32R) for s in range(RING)]
        x = sb("x", [P, T, D])
        xg = sb("x_gained", [P, T, D])
        xt_hi = sb("xt_hi", [P, KC, SEQ], F32R)
        xt_lo = sb("xt_lo", [P, KC, SEQ], F32R)
        scratch = sb("scratch", [P, 4, BANK])
        gain = [sb(f"gain{i}", [P, D]) for i in range(2)]
        square_sums = sb("square_sums", [P, 4])
        mean_sq = sb("mean_sq", [P, T])
        rms = sb("rms", [P, T])
        rstd = sb("rstd", [P, T])
        ident = sb("ident", [P, P])
        ones = sb("ones", [P, P])
        neg_ones = sb("neg_ones", [P, P])
        neg_later = sb("neg_later", [P, P])
        causal = sb("causal", [P, P])
        head_mean = sb("head_mean", [P, P])
        eps_col = sb("eps_col", [P, 1])
        inv_count = sb("inv_count", [P, 2, SEQ])
        silu = sb("silu", [P, T, GROUP])
        gated = sb("gated", [P, T, GROUP])
        gt_hi = sb("gt_hi", [P, 2, T, P], F32R)
        gt_lo = sb("gt_lo", [P, 2, T, P], F32R)
        param_rows = sb("param_rows", [P, P])
        par = sb("param_cols", [P, ROWS])
        tiny = sb("tiny", [P, 8, LC])
        half_scale = sb("half_scale", [P, LC])
        log_scale = sb("log_scale", [P, LC])
        qk_gain = sb("qk_gain", [P, 1])
        diag = sb("diag_rstd", [P, SEQ])
        rrow = sb("rstd_rows", [P, SEQ])
        qk = sb("qk", [P, 6, SEQ])
        qk_sq = xg[:, :, :].rearrange("p t d -> p (t d)")[:, 0:6 * SEQ].rearrange("p (c n) -> p c n", c=6)
        v = sb("v", [P, T, D_SB])
        HB = 3
        logs = [sb(f"logs{i}", [P, 3 * P]) for i in range(HB)]
        soft = [sb(f"soft{i}", [P, 3 * P]) for i in range(HB)]
        lbeta = [sb(f"lbeta{i}", [P, 3 * P]) for i in range(HB)]
        xpad = sb("xb_padded", [P, LC, TAPS - 1 + SEQ])
        xconv = sb("xconv", [P, LC, SEQ])
        gb = sb("gb", [P, LC, SEQ])
        gates = scratch[:, :, :].rearrange("p q n -> p (q n)")[:, 0:2 * D_LRU // P * SEQ] \
            .rearrange("p (g c n) -> p g c n", g=2, c=LC)
        r_gate, i_gate = gates[:, 0], gates[:, 1]
        th = sb("tanh_half", [P, LC, SEQ])
        rec = sb("rec", [P, LC, SEQ])
        decay = sb("decay", [P, LC, SEQ])
        PADW = max(WINDOWS)
        xc_pad = sb("xc_padded", [P, 2, PADW + SEQ])
        sums = [sb(f"sum{w}", [P, 2, PADW + SEQ]) for w in WINDOWS[:2]]
        sums += [sb(f"sum{w}", [P, 1, PADW + SEQ]) for w in WINDOWS[2:]]
        pooled = sb("pooled", [P, 2, SEQ])
        count_i = pooled[:, :, :].bitcast(I32)
        bd_a = sb("bd_a", [P, LC, P])
        bd_x = sb("bd_x", [P, LC, P])
        bd_p = sb("bd_p", [P, 2, P])
        mix_hi = sb("mix_hi", [P, KC, SEQ], F32R)
        mix_lo = sb("mix_lo", [P, KC, SEQ], F32R)
        pl = qk[:, 0:T, :]
        pt_hi, pt_lo = mix_hi[:, 0:PLE // P, :], mix_lo[:, 0:PLE // P, :]

        acc = [ctx.enter_context(nc.psum_tensor(f"acc{i}", [P, BANK], F32)) for i in range(4)]
        up = [ctx.enter_context(nc.psum_tensor(f"up{i}", [P, BANK], F32)) for i in range(T)]
        turn = [ctx.enter_context(nc.psum_tensor(f"turn{i}", [P, BANK], F32)) for i in range(2)]

        slot_loaded = [sem(f"slot_loaded{s}") for s in range(RING)]
        hi_split = sem("hi_split")
        lo_split = sem("lo_split")
        pool_split_lo = sem("pool_split_lo")
        unit_used = sem("unit_used")
        x_loaded = sem("x_loaded")
        gain_loaded = [sem(f"gain_loaded{i}") for i in range(2)]
        params_loaded = sem("params_loaded")
        p_loaded = sem("p_loaded")
        consts_ready = sem("consts_ready")
        pool_step = sem("pool_step")
        dve_step = sem("dve_step")
        act_step = sem("act_step")
        acc_ready = sem("acc_ready")
        gained = sem("gained")
        xt_turned = sem("xt_turned")
        xt_rounded = sem("xt_rounded")
        xt_split = sem("xt_split")
        squares_summed = sem("squares_summed")
        mean_ready = sem("mean_ready")
        rms_ready = sem("rms_ready")
        rstd_ready = sem("rstd_ready")
        up_ready = sem("up_ready")
        silu_ready = sem("silu_ready")
        gated_ready = sem("gated_ready")
        g_turned = sem("g_turned")
        gt_rounded = sem("gt_rounded")
        gt_split = sem("gt_split")
        params_turned = sem("params_turned")
        params_ready = sem("params_ready")
        lam_exp_ready = sem("lam_exp_ready")
        diag_ready = sem("diag_ready")
        rrow_turned = sem("rrow_turned")
        rrow_ready = sem("rrow_ready")
        qk_scaled = sem("qk_scaled")
        qk_squared = sem("qk_squared")
        qk_summed = sem("qk_summed")
        qk_rstd = sem("qk_rstd")
        qk_normed = sem("qk_normed")
        v_ready = sem("v_ready")
        z_ready = sem("z_ready")
        log_ready = sem("log_ready")
        keep_ready = sem("keep_ready")
        suffix_ready = sem("suffix_ready")
        logw_ready = sem("logw_ready")
        w_exped = sem("w_exped")
        w_ready = sem("w_ready")
        o_ready = sem("o_ready")
        o_rounded = sem("o_rounded")
        att_split = sem("att_split")
        evacuated = sem("evacuated")
        conv_ready = sem("conv_ready")
        gates_product = sem("gates_product")
        root_ready = sem("root_ready")
        gelu_ready = sem("gelu_ready")
        lru_ready = sem("lru_ready")
        lru_rounded = sem("lru_rounded")
        lru_split = sem("lru_split")
        pooled_ready = sem("pooled_ready")
        pool_product = sem("pool_product")
        pool_rounded = sem("pool_rounded")
        pool_split = sem("pool_split")
        p_turned = sem("p_turned")
        p_rounded = sem("p_rounded")
        p_split = sem("p_split")
        sig_ready = sem("sig_ready")
        decay_ready = sem("decay_ready")
        gates_ready = sem("gates_ready")
        exp_ready = sem("exp_ready")
        inverse_ready = sem("inverse_ready")
        x_done = sem("x_done")
        stored = sem("stored")

        block = ctx.enter_context(nc.Block())

        def unit_count(layer, offset, j=0):
            return layer * UNITS + offset + RING * j + 1

        def wait_split(engine, layer, offset, j=0):
            first = offset + RING * (j if isinstance(j, int) else 1)
            before = sum(n < first for n in POOL_UNITS)
            if first in POOL_UNITS:
                engine.wait_ge(pool_split_lo, layer * len(POOL_UNITS) + before + 1)
            else:
                engine.wait_ge(lo_split, layer * DVE_UNITS + offset - before + RING * j + 1 + RING)

        def unit_width(offset):
            return 4 * D_SB if offset - U_MIX in V else UNIT

        def slot_use(layer, offset, j=0):
            return layer * USES + offset // RING + j + 1

        def wait_unit(engine, layer, offset, j=0):
            engine.wait_ge(unit_used, unit_count(layer, offset, j) + RING)

        def wait_quarter(engine, layer, i, q, last_unit):
            if q < 3:
                engine.wait_ge(acc_ready, layer * 12 + 3 * i + q + 1)
            else:
                wait_unit(engine, layer, last_unit)

        def up_product_ready(engine, layer, f, base, j, t):
            if t == 0:
                engine.wait_ge(up_ready, layer * 2 * GROUPS + f * GROUPS + j + 1)
            else:
                wait_unit(engine, layer, base + (1 if isinstance(j, int) else 0),
                          0 if isinstance(j, int) else j)

        PHASE_ENDS = (U_MIX - 1, U_FFN2 - 1, U_PLE - 1, UNITS - 1)
        head_bank = [up[0], up[1], turn[1]]
        proj_bank = [up[0], up[1], turn[0], turn[1]]
        ACT_STEPS, DVE_STEPS, CONSTS = 17, 57, 28

        @block.sync
        def _(sp):
            sp.dma_start(x[:, :, :], x_in[0].rearrange("(t p) d -> p t d", p=P)).then_inc(x_loaded, 16)

            def load(layer, offset, parts, j=0):
                wait_split(sp, layer, offset - RING, j)
                for dst, src in parts:
                    sp.dma_start(dst, src).then_inc(slot_loaded[offset % RING], 16)

            def load_up(layer, offset, half, g, w1, w3, j=0):
                ks = slice(4 * half, 4 * half + 4)
                dst = raw[offset % RING][:, :].rearrange("p (k m n) -> p k m n", k=4, m=2)
                load(layer, offset, [
                    (dst[:, :, m, :], w.rearrange("l (k p) f -> l p k f", p=P)[layer, :, ks, bass.ts(g, GROUP)])
                    for m, w in enumerate((w1, w3))], j)

            def load_rows(layer, offset, w, row0, j=0):
                dst = raw[offset % RING][:, :].rearrange("p (c n) -> p c n", c=2)
                src = w.rearrange("l (r c p) n -> l r p c n", c=2, p=P)
                load(layer, offset, [(dst[:, c, :], src[layer, row0, :, c, :]) for c in (1, 0)], j)

            def load_cols(layer, offset, col0):
                dst = raw[offset % RING][:, :].rearrange("p (k n) -> p k n", k=KC)
                src = w_in.rearrange("l (k p) n -> l p k n", p=P)
                load(layer, offset, [(dst[:, k:k + 4, :], src[layer, :, k:k + 4, col0:col0 + 256])
                                     for k in (4, 0)])

            def load_v(layer, offset, half):
                dst = raw[offset % RING][:, 0:4 * D_SB].rearrange("p (k n) -> p k n", k=4)
                src = w_in.rearrange("l (k p) n -> l p k n", p=P)
                load(layer, offset, [(dst[:, k:k + 2, :],
                                      src[layer, :, 4 * half + k:4 * half + k + 2, 2 * D_SB:3 * D_SB])
                                     for k in (0, 2)])

            def load_gain(layer, i, source):
                sp.dma_start(gain[i % 2][:, :], source[bass.ds(layer, 1), :].to_broadcast([P, D])
                             ).then_inc(gain_loaded[i % 2], 16)

            def load_params(layer):
                for row, src in (
                    (ROW_CONV_W, conv_w.rearrange("l w (c p) -> l (w c) p", p=P)),
                    (ROW_CONV_B, conv_b.rearrange("l (c p) -> l c p", p=P)),
                    (ROW_BA, lru_ba.rearrange("l (c p) -> l c p", p=P)),
                    (ROW_BX, lru_bx.rearrange("l (c p) -> l c p", p=P)),
                    (ROW_LAM, lru_lambda.rearrange("l (c p) -> l c p", p=P)),
                    (ROW_SCALE, pool_scale.rearrange("l (c p) -> l c p", p=P)),
                ):
                    sp.dma_start(param_rows[row:row + src.shape[1], :], src[layer]).then_inc(params_loaded, 16)
                for row, src in ((ROW_QN, q_norm), (ROW_KN, k_norm)):
                    for b in range(2):
                        sp.dma_start(param_rows[row:row + 1, b * DH:(b + 1) * DH],
                                     src[bass.ds(layer, 1), :]).then_inc(params_loaded, 16)
                for bd, src in ((bd_a, lru_wa), (bd_x, lru_wx), (bd_p, pool_w)):
                    for b in range(2):
                        blk = slice(b * DH, (b + 1) * DH)
                        sp.dma_start(bd[blk, :, blk], src.rearrange("l (c b) i j -> l b i c j", b=2)[layer, b]
                                     ).then_inc(params_loaded, 16)

            def load_ffn(layer, base, w1, w3, w2, after_first, before_last):
                load_up(layer, base, 0, 0, w1, w3)
                load_up(layer, base + 1, 1, 0, w1, w3)
                after_first()
                with sp.Fori(1, GROUPS) as j:
                    load_up(layer, base - 1, 0, j, w1, w3, j)
                    load_up(layer, base, 1, j, w1, w3, j)
                    load_rows(layer, base + 1, w2, j - 1, j)
                before_last()
                load_rows(layer, base - 1, w2, GROUPS - 1, GROUPS)

            sp.wait_ge(consts_ready, CONSTS)
            with sp.Fori(0, DEPTH) as layer:
                def first_gains():
                    load_gain(layer, 0, ffn1_norm)
                    load_gain(layer, 1, mix_norm)

                def embeddings():
                    sp.dma_start(pl[:, :, :], p_in.rearrange("l b (t p) e -> l p (b t) e", p=P)[layer]
                                 ).then_inc(p_loaded, 16)

                load_ffn(layer, U_FFN1, ffn1_w1, ffn1_w3, ffn1_w2, first_gains, lambda: load_params(layer))
                load_gain(layer, 2, ffn2_norm)
                load_v(layer, U_MIX + V[0], 0)
                for n in range(3):
                    load_cols(layer, U_MIX + QK + n, 256 * n)
                load_v(layer, U_MIX + V[1], 1)
                for n, part in enumerate(XGC_COLS):
                    load_cols(layer, U_MIX + XGC + n, 3 * D_SB + 256 * part)
                for n, row in enumerate(WO_ROWS):
                    load_rows(layer, U_MIX + WO + n, w_out, row)
                load_gain(layer, 3, ple_norm)
                load_ffn(layer, U_FFN2, ffn2_w1, ffn2_w3, ffn2_w2, lambda: None, embeddings)
                load_rows(layer, U_PLE, ple_proj, 0)
                for n in range(4):
                    load_rows(layer, U_PLE + 1 + n, ple_gate_w, n)
            for q in range(4):
                t, cols = q // 2, slice(q % 2 * BANK, (q % 2 + 1) * BANK)
                sp.wait_ge(x_done, 4 * (DEPTH - 1) + q + 1)
                sp.dma_start(out[0, t * P:(t + 1) * P, cols], x[:, t, cols]).then_inc(stored, 16)
            sp.wait_ge(stored, 16 * 4)

        @block.gpsimd
        def _(pool):
            made = [0]

            def link(instruction):
                instruction.then_inc(consts_ready, 1)
                made[0] += 1

            def settle():
                pool.wait_ge(consts_ready, made[0])

            for tile, value in ((ident, 0.0), (ones, 1.0), (neg_ones, -1.0), (neg_later, -1.0),
                                (causal, 1.0), (head_mean, 0.0), (eps_col, EPS), (param_rows, 0.0)):
                link(nc.gpsimd.memset(tile[:, :], value))
            for tile in (xpad, xc_pad, bd_a, bd_x, bd_p, sums[0], sums[1], sums[2], sums[3]):
                link(nc.gpsimd.memset(tile[:, :, :], 0.0))
            link(nc.gpsimd.iota(count_i[:, :, :], pattern=[[0, 2], [1, SEQ]], base=1, channel_multiplier=0))
            settle()
            link(nc.gpsimd.tensor_copy(inv_count[:, :, :], count_i[:, :, :]))
            link(nc.gpsimd.affine_select(out=ident[:, :], in_=ident[:, :], compare_op=ALU.not_equal, fill=1.0,
                                         base=0, pattern=[[-1, P]], channel_multiplier=1))
            link(nc.gpsimd.affine_select(out=neg_later[:, :], in_=neg_later[:, :], compare_op=ALU.is_gt,
                                         fill=0.0, base=0, pattern=[[-1, P]], channel_multiplier=1))
            link(nc.gpsimd.affine_select(out=causal[:, :], in_=causal[:, :], compare_op=ALU.is_gt,
                                         fill=0.0, base=0, pattern=[[1, P]], channel_multiplier=-1))
            for b in range(P // DH):
                settle()
                blk = slice(b * DH, (b + 1) * DH)
                link(nc.gpsimd.memset(head_mean[blk, blk], 1.0 / DH))
            for n, w in enumerate(WINDOWS):
                settle()
                blk = slice((n % 2) * DH, (n % 2 + 1) * DH)
                link(nc.gpsimd.tensor_scalar(inv_count[blk, n // 2, :], inv_count[blk, n // 2, :],
                                             float(w), None, ALU.min))

            assert made[0] == CONSTS

            with pool.Fori(0, DEPTH) as layer:
                def split(offset):
                    slot = offset % RING
                    pool.wait_ge(hi_split, unit_count(layer, offset))
                    nc.gpsimd.tensor_tensor(wlo[slot][:, :], raw[slot][:, :], whi[slot][:, :].bitcast(F32),
                                            ALU.subtract).then_inc(pool_split_lo, 1)

                step = Steps(pool, pool_step, 8)
                step.start_layer(layer)
                for n in POOL_SPLITS:
                    split(U_MIX + n)
                pool.wait_ge(evacuated, layer * 4 + 3)
                pool.wait_ge(inverse_ready, 1)
                source, width = xc_pad, 1
                for n, total in enumerate(sums):
                    chunks = slice(0, 2) if n < 2 else slice(1, 2)
                    here = slice(0, 2) if n < 2 else slice(0, 1)
                    src = source[:, chunks, :] if n <= 2 else source[:, 0:1, :]
                    lo = 2 * width - 1 if n < 3 else PADW
                    step.done(nc.gpsimd.tensor_tensor(total[:, here, lo:], src[:, :, lo:],
                                                      src[:, :, lo - width:PADW + SEQ - width], ALU.add))
                    step.settle()
                    source, width = total, 2 * width
                for n, total in enumerate(sums):
                    blk = slice((n % 2) * DH, (n % 2 + 1) * DH)
                    step.done(nc.gpsimd.tensor_tensor(pooled[blk, n // 2, :], total[blk, 0, PADW:],
                                                      inv_count[blk, n // 2, :], ALU.mult))
                    step.settle()
                nc.gpsimd.tensor_tensor(pooled[:, :, :], pooled[:, :, :], xc_pad[:, :, PADW:],
                                        ALU.subtract).then_inc(pooled_ready, 1)
                step.end_layer()

        @block.scalar
        def _(act):
            act.wait_ge(consts_ready, CONSTS)
            with act.Fori(0, DEPTH) as layer:
                step = Steps(act, act_step, ACT_STEPS)
                step.start_layer(layer)

                def split(offset, j=0):
                    slot = offset % RING
                    width = unit_width(offset)
                    act.wait_ge(slot_loaded[slot], 16 * HALVES * slot_use(layer, offset, j))
                    act.wait_ge(unit_used, unit_count(layer, offset, j))
                    nc.scalar.activation(whi[slot][:, 0:width], raw[slot][:, 0:width], ACT.Copy
                                         ).then_inc(hi_split, 1)

                def norm(i, unit_between=None):
                    for q in range(4):
                        t, h = q // 2, q % 2
                        act.wait_ge(xt_turned, layer * 16 + 4 * i + q + 1)
                        nc.scalar.activation(xt_hi[:, 4 * h:4 * h + 4, t * P:(t + 1) * P],
                                             acc[q][:, :].rearrange("p (k n) -> p k n", k=4),
                                             ACT.Copy).then_inc(xt_rounded, 1)
                    if unit_between is not None:
                        split(unit_between)
                    for q in range(4):
                        t, h = q // 2, q % 2
                        last = nc.scalar.activation(scratch[:, q, :], x[:, t, h * BANK:(h + 1) * BANK],
                                                    ACT.Square, accum_out=square_sums[:, q:q + 1])
                    last.then_inc(squares_summed, 1)
                    act.wait_ge(mean_ready, layer * 4 + i + 1)
                    nc.scalar.activation(rms[:, :], mean_sq[:, :], ACT.Sqrt, bias=eps_col[:, :],
                                         scale=1.0 / D).then_inc(rms_ready, 1)

                def ffn(f, i, base):
                    def silus(j):
                        for t in range(T):
                            up_product_ready(act, layer, f, base, j, t)
                            nc.scalar.activation(silu[:, t, :], up[t][:, 0:GROUP], ACT.Silu,
                                                 scale=rstd[:, t:t + 1]).then_inc(silu_ready, 1)

                    def round_gt(j):
                        act.wait_ge(g_turned, layer * 2 * GROUPS + f * GROUPS + j + 1)
                        nc.scalar.activation(gt_hi[:, :, :, :],
                                             turn[0][:, :].rearrange("p (c t n) -> p c t n", c=2, t=T),
                                             ACT.Copy).then_inc(gt_rounded, 1)

                    split(base + 2)
                    act.wait_ge(rstd_ready, layer * 4 + i + 1)
                    silus(0)
                    split(base + 3)
                    round_gt(0)
                    with act.Fori(1, GROUPS) as j:
                        split(base + 1, j=j)
                        split(base + 2, j=j)
                        act.wait_ge(gated_ready, layer * 4 * GROUPS + (f * GROUPS + j) * 2)
                        silus(j)
                        split(base + 3, j=j)
                        round_gt(j)

                def params():
                    act.wait_ge(params_turned, layer + 1)
                    nc.scalar.activation(par[:, :], turn[1][:, 0:ROWS], ACT.Copy).then_inc(params_ready, 1)
                    act.wait_ge(params_ready, layer + 1)
                    step.done(nc.scalar.activation(tiny[:, 0, :], par[:, ROW_LAM:ROW_LAM + LC], ACT.Abs))
                    step.settle()
                    nc.scalar.activation(tiny[:, 1, :], tiny[:, 0, :], ACT.Exp, scale=-1.0
                                         ).then_inc(lam_exp_ready, 1)

                split(U_FFN1)
                split(U_FFN1 + 1)
                norm(0)
                ffn(0, 0, U_FFN1)
                split(U_MIX + 1)

                norm(1, U_MIX + 2)
                split(U_MIX + 3)
                params()
                split(U_MIX + 4)
                act.wait_ge(rrow_turned, layer + 1)
                nc.scalar.activation(rrow[:, :], turn[1][:, 0:SEQ], ACT.Copy).then_inc(rrow_ready, 1)
                for g in range(3):
                    act.wait_ge(qk_scaled, layer * 3 + g + 1)
                    nc.scalar.activation(qk_sq[:, 2 * g:2 * g + 2, :], qk[:, 2 * g:2 * g + 2, :],
                                         ACT.Square).then_inc(qk_squared, 1)
                    if g < 2:
                        split(U_MIX + 5 + g)
                for g, bank in enumerate((turn[0], turn[1], acc[3])):
                    act.wait_ge(qk_summed, layer * 3 + g + 1)
                    step.done(nc.scalar.activation(qk_sq[:, 2 * g:2 * g + 2, :],
                                                   bank[:, :].rearrange("p (c n) -> p c n", c=2),
                                                   ACT.Ln, bias=eps_col[:, :]))
                step.settle()
                for g in range(3):
                    nc.scalar.activation(qk_sq[:, 2 * g:2 * g + 2, :], qk_sq[:, 2 * g:2 * g + 2, :],
                                         ACT.Exp, scale=-0.5).then_inc(qk_rstd, 1)

                def head_logs(first):
                    for h in range(first, first + HB):
                        act.wait_ge(z_ready, layer * HEADS + h + 1)
                        step.done(nc.scalar.activation(logs[h % HB][:, :], head_bank[h % HB][:, 0:3 * P], ACT.Abs))
                    step.settle()
                    for h in range(first, first + HB):
                        step.done(nc.scalar.activation(logs[h % HB][:, :], logs[h % HB][:, :], ACT.Exp, scale=-1.0))
                    step.settle()
                    for h in range(first, first + HB):
                        nc.scalar.activation(logs[h % HB][:, :], logs[h % HB][:, :], ACT.Ln, bias=ones[:, 0:1]
                                             ).then_inc(log_ready, 1)

                def head_weights(first):
                    for h in range(first, first + HB):
                        act.wait_ge(logw_ready, layer * HEADS + h + 1)
                        nc.scalar.activation(lbeta[h % HB][:, :], lbeta[h % HB][:, :], ACT.Exp
                                             ).then_inc(w_exped, 1)

                def round_o(c):
                    act.wait_ge(o_ready, layer * HEADS + 2 * c + 2)
                    nc.scalar.activation(mix_hi[:, c, :], turn[0][:, 0:SEQ], ACT.Copy).then_inc(o_rounded, 1)

                def lru_gates():
                    for c in range(LC):
                        act.wait_ge(gates_product, layer * LC + c + 1)
                        nc.scalar.activation(r_gate[:, c, :], acc[c][:, 0:SEQ], ACT.Sigmoid,
                                             bias=par[:, ROW_BA + c:ROW_BA + c + 1])
                        last = nc.scalar.activation(i_gate[:, c, :], acc[c][:, SEQ:2 * SEQ], ACT.Sigmoid,
                                                    bias=par[:, ROW_BX + c:ROW_BX + c + 1])
                    last.then_inc(gates_ready, 1)

                def lru_decay():
                    act.wait_ge(gates_ready, layer + 1)
                    act.wait_ge(decay_ready, layer + 1)
                    for c in range(LC):
                        last = nc.scalar.activation(decay[:, c, :], r_gate[:, c, :], ACT.Exp,
                                                    scale=log_scale[:, c:c + 1])
                    last.then_inc(exp_ready, 1)

                def lru_root():
                    for c in range(LC):
                        last = nc.scalar.activation(th[:, c, :], r_gate[:, c, :], ACT.Tanh,
                                                    scale=half_scale[:, c:c + 1])
                    step.done(last)
                    step.settle()
                    nc.scalar.activation(r_gate[:, :, :], th[:, :, :], ACT.Sqrt, scale=-1.0
                                         ).then_inc(root_ready, 1)

                def gelu():
                    act.wait_ge(evacuated, layer * 4 + 4)
                    nc.scalar.activation(gb[:, :, :], gb[:, :, :], ACT.Gelu_apprx_tanh).then_inc(gelu_ready, 1)

                def round_pool():
                    act.wait_ge(pool_product, layer + 1)
                    for c in range(2):
                        last = nc.scalar.activation(mix_hi[:, KC - 2 + c, :], acc[3][:, c * SEQ:(c + 1) * SEQ],
                                                    ACT.Copy, scale=par[:, ROW_SCALE + c:ROW_SCALE + c + 1])
                    last.then_inc(pool_rounded, 1)

                def round_lru():
                    act.wait_ge(lru_ready, layer + 1)
                    nc.scalar.activation(mix_hi[:, 3:6, :], gb[:, :, :], ACT.Copy).then_inc(lru_rounded, 1)

                split(U_MIX + 7)
                head_logs(0)
                split(U_MIX + 8)
                split(U_MIX + 9)
                head_weights(0)
                split(U_MIX + 10)
                head_logs(3)
                round_o(0)
                lru_gates()
                round_pool()
                split(U_MIX + 11)
                lru_decay()
                head_weights(3)
                lru_root()
                gelu()
                round_o(1)
                round_o(2)
                split(U_MIX + 12)
                round_lru()
                split(U_FFN2)
                split(U_FFN2 + 1)

                norm(2)
                ffn(1, 2, U_FFN2)
                act.wait_ge(p_turned, layer + 1)
                nc.scalar.activation(pt_hi[:, :, :], turn[1][:, :].rearrange("p (c n) -> p c n", c=2),
                                     ACT.Copy).then_inc(p_rounded, 1)
                split(U_PLE + 1)

                split(U_PLE + 2)
                norm(3)
                split(U_PLE + 3)
                split(U_PLE + 4)
                act.wait_ge(rstd_ready, layer * 4 + 4)
                for q in range(4):
                    t = q // 2
                    wait_quarter(act, layer, 3, q, UNITS - 1)
                    nc.scalar.activation(scratch[:, q, :], acc[q][:, :], ACT.Sigmoid,
                                         scale=rstd[:, t:t + 1]).then_inc(sig_ready, 1)
                step.end_layer()

        @block.vector
        def _(dve):
            nc.vector.memset(square_sums[:, 0:1], 0.0).then_inc(lo_split, RING)
            nc.vector.memset(square_sums[:, 1:2], 0.0).then_inc(unit_used, RING)
            dve.wait_ge(consts_ready, CONSTS)
            nc.vector.reciprocal(inv_count[:, :, :], inv_count[:, :, :]).then_inc(inverse_ready, 1)
            dve.wait_ge(x_loaded, 16)
            with dve.Fori(0, DEPTH) as layer:
                step = Steps(dve, dve_step, DVE_STEPS)
                step.start_layer(layer)

                def split(offset, j=0):
                    slot = offset % RING
                    width = unit_width(offset)
                    dve.wait_ge(hi_split, unit_count(layer, offset, j))
                    nc.vector.tensor_tensor(wlo[slot][:, 0:width], raw[slot][:, 0:width],
                                            whi[slot][:, 0:width].bitcast(F32), ALU.subtract
                                            ).then_inc(lo_split, 1)

                def quarter(tile, q):
                    return tile[:, q // 2, (q % 2) * BANK:(q % 2 + 1) * BANK]

                def apply_gain(i, q):
                    nc.vector.tensor_tensor(quarter(xg, q), quarter(x, q),
                                            gain[i % 2][:, (q % 2) * BANK:(q % 2 + 1) * BANK],
                                            ALU.mult).then_inc(gained, 1)

                def residual(i, scale, q):
                    if q == 0:
                        dve.wait_ge(gain_loaded[i % 2], 16 * (layer * 2 + i // 2 + 1))
                    wait_quarter(dve, layer, i - 1, q, PHASE_ENDS[i - 1])
                    step.done(nc.vector.scalar_tensor_tensor(
                        out=quarter(x, q), in0=acc[q][:, :], scalar=scale, in1=quarter(x, q),
                        op0=ALU.mult, op1=ALU.add))
                    step.settle()
                    apply_gain(i, q)

                def split_xt(i, q):
                    t, h = q // 2, q % 2
                    dve.wait_ge(xt_rounded, layer * 16 + 4 * i + q + 1)
                    cols = (slice(None), slice(4 * h, 4 * h + 4), slice(t * P, (t + 1) * P))
                    nc.vector.tensor_tensor(xt_lo[cols], acc[q][:, :].rearrange("p (k n) -> p k n", k=4),
                                            xt_hi[cols].bitcast(F32), ALU.subtract).then_inc(xt_split, 1)

                def statistics(i):
                    dve.wait_ge(squares_summed, layer * 4 + i + 1)
                    nc.vector.tensor_tensor(mean_sq[:, :], square_sums[:, 0:4:2], square_sums[:, 1:4:2],
                                            ALU.add).then_inc(mean_ready, 1)
                    dve.wait_ge(rms_ready, layer * 4 + i + 1)
                    nc.vector.reciprocal(rstd[:, :], rms[:, :]).then_inc(rstd_ready, 1)

                def residual_norm(i, scale, next_unit):
                    for q in range(3):
                        residual(i, scale, q)
                    split_xt(i, 0)
                    residual(i, scale, 3)
                    split_xt(i, 1)
                    split_xt(i, 2)
                    split(next_unit)
                    split_xt(i, 3)

                def ffn(f, i, base):
                    def gates(j):
                        for t in range(T):
                            dve.wait_ge(silu_ready, layer * 4 * GROUPS + (f * GROUPS + j) * 2 + t + 1)
                            nc.vector.scalar_tensor_tensor(
                                out=gated[:, t, :], in0=up[t][:, GROUP:2 * GROUP], scalar=rstd[:, t:t + 1],
                                in1=silu[:, t, :], op0=ALU.mult, op1=ALU.mult).then_inc(gated_ready, 1)

                    def split_gt(j):
                        dve.wait_ge(gt_rounded, layer * 2 * GROUPS + f * GROUPS + j + 1)
                        nc.vector.tensor_tensor(gt_lo[:, :, :, :].rearrange("p c t n -> p (c t n)"), turn[0][:, :],
                                                gt_hi[:, :, :, :].bitcast(F32).rearrange("p c t n -> p (c t n)"),
                                                ALU.subtract).then_inc(gt_split, 1)

                    split(base + 2)
                    dve.wait_ge(rstd_ready, layer * 4 + i + 1)
                    gates(0)
                    split(base + 3)
                    split_gt(0)
                    with dve.Fori(1, GROUPS) as j:
                        split(base + 1, j=j)
                        split(base + 2, j=j)
                        gates(j)
                        split(base + 3, j=j)
                        split_gt(j)

                def params():
                    dve.wait_ge(lam_exp_ready, layer + 1)
                    e, den, s, s2, poly = (tiny[:, n, :] for n in (1, 2, 3, 4, 5))
                    lam = par[:, ROW_LAM:ROW_LAM + LC]

                    def link(instruction):
                        step.done(instruction)
                        step.settle()

                    link(nc.vector.tensor_scalar(den, e, 2.0, None, ALU.add))
                    link(nc.vector.reciprocal(den, den))
                    link(nc.vector.tensor_tensor(s, e, den, ALU.mult))
                    link(nc.vector.tensor_tensor(s2, s, s, ALU.mult))
                    link(nc.vector.tensor_scalar(poly, s2, 1.0 / 15, None, ALU.mult))
                    for odd in (13, 11, 9, 7, 5, 3):
                        link(nc.vector.scalar_tensor_tensor(out=poly, in0=poly, scalar=1.0 / odd, in1=s2,
                                                            op0=ALU.add, op1=ALU.mult))
                    link(nc.vector.scalar_tensor_tensor(out=poly, in0=poly, scalar=1.0, in1=s,
                                                        op0=ALU.add, op1=ALU.mult))
                    link(nc.vector.tensor_scalar(s, lam, 0.0, 4.0, ALU.min, ALU.mult))
                    link(nc.vector.scalar_tensor_tensor(out=half_scale[:, :], in0=poly, scalar=-8.0, in1=s,
                                                        op0=ALU.mult, op1=ALU.add))
                    nc.vector.tensor_scalar(log_scale[:, :], half_scale[:, :], 2.0, None, ALU.mult
                                            ).then_inc(decay_ready, 1)
                    link(nc.vector.scalar_tensor_tensor(
                        out=qk_gain[:, :], in0=par[:, ROW_QN:ROW_QN + 1], scalar=float(DH) ** -0.5,
                        in1=par[:, ROW_KN:ROW_KN + 1], op0=ALU.mult, op1=ALU.mult))

                dve.wait_ge(gain_loaded[0], 16 * (layer * 2 + 1))
                for q in range(4):
                    apply_gain(0, q)
                split(U_FFN1)
                for q in range(3):
                    split_xt(0, q)
                split(U_FFN1 + 1)
                split_xt(0, 3)
                statistics(0)
                ffn(0, 0, U_FFN1)

                residual_norm(1, 0.5, U_MIX + 1)
                split(U_MIX + 2)
                statistics(1)
                dve.wait_ge(rstd_ready, layer * 4 + 2)
                for t in range(T):
                    last = nc.vector.tensor_scalar(diag[:, t * P:(t + 1) * P], ident[:, :], rstd[:, t:t + 1],
                                                   None, ALU.mult)
                last.then_inc(diag_ready, 1)
                params()
                split(U_MIX + 3)
                rr = rrow[:, :].unsqueeze(1).to_broadcast([P, 2, SEQ])

                def chunks(bank, n=2):
                    return bank[:, :].rearrange("p (c n) -> p c n", c=2)

                dve.wait_ge(rrow_ready, layer + 1)
                for g in range(3):
                    wait_unit(dve, layer, U_MIX + QK + g)
                    nc.vector.tensor_tensor(qk[:, 2 * g:2 * g + 2, :], chunks(acc[g]), rr, ALU.mult
                                            ).then_inc(qk_scaled, 1)
                    if g == 1:
                        split(U_MIX + 5)
                wait_unit(dve, layer, U_MIX + V[1])
                for t in range(T):
                    nc.vector.tensor_scalar(v[:, t, :], up[t][:, 0:D_SB], rstd[:, t:t + 1], None, ALU.mult
                                            ).then_inc(v_ready, 1)
                for g in range(3):
                    dve.wait_ge(qk_rstd, layer * 3 + g + 1)
                    last = nc.vector.tensor_tensor(qk[:, 2 * g:2 * g + 2, :], qk[:, 2 * g:2 * g + 2, :],
                                                   qk_sq[:, 2 * g:2 * g + 2, :], ALU.mult)
                step.done(last)
                step.settle()
                nc.vector.tensor_scalar(qk[:, 0:3, :], qk[:, 0:3, :], qk_gain[:, :], None, ALU.mult
                                        ).then_inc(qk_normed, 1)

                def head_keeps(first):
                    for h in range(first, first + HB):
                        b = h % HB
                        bank = head_bank[b][:, 0:3 * P]
                        dve.wait_ge(log_ready, layer * HEADS + h + 1)
                        if h >= HB:
                            dve.wait_ge(o_ready, layer * HEADS + h - HB + 1)
                        step.done(nc.vector.scalar_tensor_tensor(out=soft[b][:, :], in0=bank, scalar=0.0,
                                                                 in1=logs[b][:, :], op0=ALU.max, op1=ALU.add))
                        step.done(nc.vector.scalar_tensor_tensor(out=lbeta[b][:, :], in0=bank, scalar=0.0,
                                                                 in1=logs[b][:, :], op0=ALU.min, op1=ALU.subtract))
                        step.settle()
                        diagonal = soft[b][:, :].rearrange("p (b c) -> p b c", b=3)[:, 0:3:2, :]
                        nc.vector.tensor_tensor(diagonal, diagonal,
                                                causal[:, :].unsqueeze(1).to_broadcast([P, 2, P]),
                                                ALU.mult).then_inc(keep_ready, 1)

                def mask_weights(first):
                    for h in range(first, first + HB):
                        dve.wait_ge(w_exped, layer * HEADS + h + 1)
                        diagonal = lbeta[h % HB][:, :].rearrange("p (b c) -> p b c", b=3)[:, 0:3:2, :]
                        nc.vector.tensor_tensor(diagonal, diagonal,
                                                causal[:, :].unsqueeze(1).to_broadcast([P, 2, P]),
                                                ALU.mult).then_inc(w_ready, 1)

                def head_sums(first):
                    for h in range(first, first + HB):
                        b = h % HB
                        dve.wait_ge(suffix_ready, layer * HEADS + h + 1)
                        nc.vector.tensor_tensor(lbeta[b][:, :], head_bank[b][:, 0:3 * P], lbeta[b][:, :],
                                                ALU.add).then_inc(logw_ready, 1)

                def split_o(c):
                    dve.wait_ge(o_rounded, layer * 3 + c + 1)
                    nc.vector.tensor_tensor(mix_lo[:, c, :], turn[0][:, 0:SEQ], mix_hi[:, c, :].bitcast(F32),
                                            ALU.subtract).then_inc(att_split, 1)

                def evacuate(n, parts):
                    wait_unit(dve, layer, U_MIX + XGC + n)
                    for dst, src, row in parts:
                        last = nc.vector.tensor_tensor(dst, src, row, ALU.mult)
                    last.then_inc(evacuated, 1)

                def convolution():
                    dve.wait_ge(evacuated, layer * 4 + 2)
                    for w in range(TAPS):
                        for c in range(LC):
                            cw = par[:, ROW_CONV_W + w * LC + c:ROW_CONV_W + w * LC + c + 1]
                            window = xpad[:, c, w:w + SEQ]
                            if w == 0:
                                last = nc.vector.tensor_scalar(xconv[:, c, :], window, cw,
                                                               par[:, ROW_CONV_B + c:ROW_CONV_B + c + 1],
                                                               ALU.mult, ALU.add)
                            else:
                                last = nc.vector.scalar_tensor_tensor(
                                    out=xconv[:, c, :], in0=window, scalar=cw, in1=xconv[:, c, :],
                                    op0=ALU.mult, op1=ALU.add)
                            if w < TAPS - 1:
                                step.done(last)
                        if w < TAPS - 1:
                            step.settle()
                    last.then_inc(conv_ready, 1)

                def recurrence():
                    dve.wait_ge(gates_ready, layer + 1)
                    step.done(nc.vector.tensor_tensor(i_gate[:, :, :], i_gate[:, :, :], xconv[:, :, :], ALU.mult))
                    dve.wait_ge(exp_ready, layer + 1)
                    dve.wait_ge(root_ready, layer + 1)
                    step.done(nc.vector.scalar_tensor_tensor(out=rec[:, :, :], in0=decay[:, :, :], scalar=1.0,
                                                             in1=r_gate[:, :, :], op0=ALU.add, op1=ALU.mult))
                    step.settle()
                    step.done(nc.vector.tensor_tensor(rec[:, :, :], rec[:, :, :], i_gate[:, :, :], ALU.mult))
                    step.settle()
                    for c in range(LC):
                        last = nc.vector.tensor_tensor_scan(th[:, c, :], decay[:, c, :], rec[:, c, :], 0.0,
                                                            ALU.mult, ALU.add)
                    step.done(last)
                    step.settle()
                    dve.wait_ge(gelu_ready, layer + 1)
                    nc.vector.tensor_tensor(gb[:, :, :], gb[:, :, :], th[:, :, :], ALU.mult).then_inc(lru_ready, 1)

                def split_pool():
                    dve.wait_ge(pool_rounded, layer + 1)
                    for c in range(2):
                        last = nc.vector.scalar_tensor_tensor(
                            out=mix_lo[:, KC - 2 + c, :], in0=acc[3][:, c * SEQ:(c + 1) * SEQ],
                            scalar=par[:, ROW_SCALE + c:ROW_SCALE + c + 1],
                            in1=mix_hi[:, KC - 2 + c, :].bitcast(F32), op0=ALU.mult, op1=ALU.subtract)
                    last.then_inc(pool_split, 1)

                def split_lru():
                    dve.wait_ge(lru_rounded, layer + 1)
                    nc.vector.tensor_tensor(mix_lo[:, 3:6, :], gb[:, :, :], mix_hi[:, 3:6, :].bitcast(F32),
                                            ALU.subtract).then_inc(lru_split, 1)

                split(U_MIX + 7)
                head_keeps(0)
                evacuate(0, [(xpad[:, 0:2, TAPS - 1:], chunks(acc[0]), rr)])
                split(U_MIX + 8)
                evacuate(1, [(xpad[:, 2, TAPS - 1:], acc[1][:, 0:SEQ], rrow[:, :]),
                             (gb[:, 0, :], acc[1][:, SEQ:2 * SEQ], rrow[:, :])])
                head_sums(0)
                evacuate(2, [(xc_pad[:, :, PADW:], chunks(acc[2]), rr)])
                convolution()
                mask_weights(0)
                evacuate(3, [(gb[:, 1:3, :], chunks(acc[3]), rr)])
                split(U_MIX + 10)
                split_o(0)
                head_keeps(3)
                split_pool()
                head_sums(3)
                split(U_MIX + 11)
                mask_weights(3)
                recurrence()
                split_o(1)
                split_o(2)
                split(U_MIX + 12)
                split_lru()
                split(U_FFN2)

                residual_norm(2, 1.0, U_FFN2 + 1)
                statistics(2)
                ffn(1, 2, U_FFN2)
                dve.wait_ge(p_rounded, layer + 1)
                nc.vector.tensor_tensor(pt_lo[:, :, :], chunks(turn[1]), pt_hi[:, :, :].bitcast(F32),
                                        ALU.subtract).then_inc(p_split, 1)

                residual_norm(3, 0.5, U_PLE + 1)
                split(U_PLE + 2)
                statistics(3)
                split(U_PLE + 3)
                split(U_PLE + 4)
                for q in range(4):
                    dve.wait_ge(sig_ready, layer * 4 + q + 1)
                    step.done(nc.vector.tensor_tensor(scratch[:, q, :], proj_bank[q][:, :], scratch[:, q, :],
                                                      ALU.mult))
                    step.settle()
                    nc.vector.tensor_tensor(quarter(x, q), quarter(x, q), scratch[:, q, :], ALU.add
                                            ).then_inc(x_done, 1)
                dve.wait_ge(x_done, 4 * layer + 4)
                step.end_layer()

        @block.tensor
        def _(pe):
            pe.wait_ge(consts_ready, CONSTS)
            with pe.Fori(0, DEPTH) as layer:
                def unit_split(offset, j=0):
                    wait_split(pe, layer, offset, j)

                def three(bank, a_hi, a_lo, b_hi, b_lo, start, stop):
                    nc.tensor.matmul(bank, a_hi, b_hi, start=start, stop=False)
                    nc.tensor.matmul(bank, a_hi, b_lo, start=False, stop=False)
                    return nc.tensor.matmul(bank, a_lo, b_hi, start=False, stop=stop)

                def turn_x(i, q):
                    t, h = q // 2, q % 2
                    pe.wait_ge(gained, layer * 16 + 4 * i + q + 1)
                    for k in range(4):
                        last = nc.tensor.transpose(acc[q][:, k * P:(k + 1) * P],
                                                   xg[:, t, (4 * h + k) * P:(4 * h + k + 1) * P], ident[:, :])
                    last.then_inc(xt_turned, 1)

                def xt_wait(i, half, t):
                    pe.wait_ge(xt_split, layer * 16 + 4 * i + 2 * t + half + 1)

                def rows_unit(offset, a_hi, a_lo, chunks, banks, first=False, last_of=None, j=0, stop=False):
                    slot = offset % RING
                    unit_split(offset, j)
                    ends = last_of is not None
                    order = [(c, t, h) for c in range(2) for t in range(T) for h in range(2)]
                    if ends:
                        order.sort(key=lambda x: (2 * x[1] + x[2], x[0]))
                    for c, t, h in order:
                        q = 2 * t + h
                        if ends and last_of < 4 and (q, c) == (3, 0):
                            turn_x(last_of, 0)
                        cols = slice(c * D + h * BANK, c * D + (h + 1) * BANK)
                        last = three(banks[q][:, :], a_hi(chunks[c], t), a_lo(chunks[c], t),
                                     whi[slot][:, cols], wlo[slot][:, cols],
                                     start=first and c == 0, stop=(ends or stop) and c == 1)
                        if ends and c == 1 and q < 3:
                            last.then_inc(acc_ready, 1)
                    last.then_inc(unit_used, 1)
                    if ends and last_of < 4:
                        turn_x(last_of, 1)
                        turn_x(last_of, 2)

                def of(tile):
                    return lambda k, t: tile[:, k, t * P:(t + 1) * P]

                def ffn(f, i, base, before_last):
                    def up_group(offset, j, norm=None):
                        for half in range(2):
                            o = offset + half
                            slot = o % RING
                            unit_split(o, j)
                            for t in range(T):
                                if norm is not None:
                                    if (half, t) == (0, 1):
                                        turn_x(norm, 3)
                                    xt_wait(norm, half, t)
                                for kk in range(4):
                                    k = 4 * half + kk
                                    cols = slice(kk * BANK, (kk + 1) * BANK)
                                    last = three(up[t][:, :], of(xt_hi)(k, t), of(xt_lo)(k, t),
                                                 whi[slot][:, cols], wlo[slot][:, cols],
                                                 start=k == 0, stop=k == KC - 1)
                                if half == 1 and t == 0:
                                    last.then_inc(up_ready, 1)
                            last.then_inc(unit_used, 1)

                    def turn_g(g):
                        pe.wait_ge(gated_ready, layer * 4 * GROUPS + (f * GROUPS + g) * 2 + 2)
                        for c in range(2):
                            for t in range(T):
                                last = nc.tensor.transpose(turn[0][:, (c * T + t) * P:(c * T + t + 1) * P],
                                                           gated[:, t, c * P:(c + 1) * P], ident[:, :])
                        last.then_inc(g_turned, 1)

                    def down(offset, j, g, first, last_of=None):
                        pe.wait_ge(gt_split, layer * 2 * GROUPS + f * GROUPS + g + 1)
                        rows_unit(offset, lambda c, t: gt_hi[:, c, t, :], lambda c, t: gt_lo[:, c, t, :],
                                  (0, 1), acc, first, last_of, j)

                    up_group(base, 0, i)
                    turn_g(0)
                    up_group(base - 1, 1)
                    down(base + 1, 1, 0, True)
                    turn_g(1)
                    with pe.Fori(2, GROUPS) as j:
                        up_group(base - 1, j)
                        down(base + 1, j, j - 1, False)
                        turn_g(j)
                    before_last()
                    down(base - 1, GROUPS, GROUPS - 1, False, i + 1)

                def turn_params():
                    pe.wait_ge(params_loaded, 16 * PARAM_DMAS * (layer + 1))
                    nc.tensor.transpose(turn[1][:, 0:P], param_rows[:, :], ident[:, :]
                                        ).then_inc(params_turned, 1)

                def turn_p():
                    pe.wait_ge(p_loaded, 16 * (layer + 1))
                    for c in range(2):
                        for t in range(T):
                            last = nc.tensor.transpose(turn[1][:, (c * T + t) * P:(c * T + t + 1) * P],
                                                       pl[:, t, c * P:(c + 1) * P], ident[:, :])
                    last.then_inc(p_turned, 1)

                for q in range(3):
                    turn_x(0, q)
                ffn(0, 0, U_FFN1, turn_params)

                def features(n, bank, between=None):
                    slot = (U_MIX + n) % RING
                    unit_split(U_MIX + n)
                    for c in range(2):
                        if c == 1 and between is not None:
                            between()
                        out_ = bank[:, c * SEQ:(c + 1) * SEQ]
                        for k in range(KC):
                            cols = slice(k * 256 + c * P, k * 256 + (c + 1) * P)
                            nc.tensor.matmul(out_, whi[slot][:, cols], xt_hi[:, k, :], start=k == 0, stop=False)
                            nc.tensor.matmul(out_, whi[slot][:, cols], xt_lo[:, k, :], start=False, stop=False)
                            last = nc.tensor.matmul(out_, wlo[slot][:, cols], xt_hi[:, k, :], start=False,
                                                    stop=k == KC - 1)
                    last.then_inc(unit_used, 1)

                def head_z(h):
                    if h == 0:
                        pe.wait_ge(qk_normed, layer + 1)
                        pe.wait_ge(v_ready, layer * T + T)
                    if h >= HB:
                        pe.wait_ge(logw_ready, layer * HEADS + h - HB + 1)
                    rows, c, bank = slice(h % 2 * DH, (h % 2 + 1) * DH), h // 2, head_bank[h % HB]
                    nc.tensor.matmul(bank[:, 0:2 * P], qk[rows, 3 + c, 0:P], qk[rows, c, :], start=True, stop=True)
                    nc.tensor.matmul(bank[:, 2 * P:3 * P], qk[rows, 3 + c, P:2 * P], qk[rows, c, P:2 * P],
                                     start=True, stop=True).then_inc(z_ready, 1)

                def head_suffix(h):
                    pe.wait_ge(keep_ready, layer * HEADS + h + 1)
                    bank = head_bank[h % HB]
                    nc.tensor.matmul(bank[:, 0:3 * P], neg_later[:, :], soft[h % HB][:, :], start=True, stop=False)
                    nc.tensor.matmul(bank[:, P:2 * P], neg_ones[:, :], soft[h % HB][:, 2 * P:3 * P],
                                     start=False, stop=True).then_inc(suffix_ready, 1)

                def lru_gate_products():
                    pe.wait_ge(conv_ready, layer + 1)
                    for c in range(LC):
                        nc.tensor.matmul(acc[c][:, 0:SEQ], bd_a[:, c, :], xconv[:, c, :], start=True, stop=True)
                        nc.tensor.matmul(acc[c][:, SEQ:2 * SEQ], bd_x[:, c, :], xconv[:, c, :],
                                         start=True, stop=True).then_inc(gates_product, 1)

                def pool_products():
                    pe.wait_ge(pooled_ready, layer + 1)
                    pe.wait_ge(evacuated, layer * 4 + 4)
                    for c in range(2):
                        last = nc.tensor.matmul(acc[3][:, c * SEQ:(c + 1) * SEQ], bd_p[:, c, :],
                                                pooled[:, c, :], start=True, stop=True)
                    last.then_inc(pool_product, 1)

                def head_out(h):
                    pe.wait_ge(w_ready, layer * HEADS + h + 1)
                    if h % 2 == 0 and h >= 2:
                        pe.wait_ge(att_split, layer * 3 + h // 2)
                    rows, cols = slice(h % 2 * DH, (h % 2 + 1) * DH), slice(h * DH, (h + 1) * DH)
                    nc.tensor.matmul(turn[0][rows, 0:2 * P], v[:, 0, cols], lbeta[h % HB][:, 0:2 * P],
                                     start=True, stop=False)
                    nc.tensor.matmul(turn[0][rows, P:2 * P], v[:, 1, cols], lbeta[h % HB][:, 2 * P:3 * P],
                                     start=False, stop=True).then_inc(o_ready, 1)

                def values(half):
                    slot = (U_MIX + V[half]) % RING
                    unit_split(U_MIX + V[half])
                    for t in range(T):
                        if half == 0:
                            if t == 1:
                                turn_x(1, 3)
                            xt_wait(1, 0, t)
                        for kk in range(4):
                            k = 4 * half + kk
                            cols = slice(kk * D_SB, (kk + 1) * D_SB)
                            last = three(up[t][:, 0:D_SB], of(xt_hi)(k, t), of(xt_lo)(k, t),
                                         whi[slot][:, cols], wlo[slot][:, cols], start=k == 0, stop=k == KC - 1)
                    last.then_inc(unit_used, 1)

                def head_means(g, bank):
                    pe.wait_ge(qk_squared, layer * 3 + g + 1)
                    nc.tensor.matmul(bank[:, :], head_mean[:, :], qk_sq[:, 2 * g:2 * g + 2, :],
                                     start=True, stop=True).then_inc(qk_summed, 1)

                def three_heads(part, first):
                    for h in range(first, first + HB):
                        part(h)

                values(0)
                xt_wait(1, 1, 1)
                features(QK, acc[0])
                pe.wait_ge(diag_ready, layer + 1)
                pe.wait_ge(params_ready, layer + 1)
                nc.tensor.matmul(turn[1][:, 0:SEQ], ones[:, :], diag[:, :], start=True, stop=True
                                 ).then_inc(rrow_turned, 1)
                features(QK + 1, acc[1])
                features(QK + 2, acc[2])
                head_means(0, turn[0])
                pe.wait_ge(rrow_ready, layer + 1)
                head_means(1, turn[1])
                values(1)
                head_means(2, acc[3])
                features(XGC, acc[0])
                three_heads(head_z, 0)
                features(XGC + 1, acc[1])
                features(XGC + 2, acc[2], lambda: three_heads(head_suffix, 0))
                features(XGC + 3, acc[3], lambda: three_heads(head_z, 3))
                head_out(0)
                head_out(1)
                lru_gate_products()
                head_out(2)
                pool_products()
                three_heads(head_suffix, 3)
                pe.wait_ge(gates_ready, layer + 1)
                pe.wait_ge(pool_split, layer + 1)
                rows_unit(U_MIX + WO, of(mix_hi), of(mix_lo), (6, 7), acc, True)
                three_heads(head_out, 3)
                for n, row in enumerate(WO_ROWS):
                    if n == 0:
                        continue
                    if row == 0:
                        pe.wait_ge(att_split, layer * 3 + 2)
                    else:
                        pe.wait_ge(lru_split, layer + 1)
                        if row == 1:
                            pe.wait_ge(att_split, layer * 3 + 3)
                    rows_unit(U_MIX + WO + n, of(mix_hi), of(mix_lo), (2 * row, 2 * row + 1), acc, False,
                              2 if n == 3 else None)

                ffn(1, 2, U_FFN2, turn_p)

                pe.wait_ge(p_split, layer + 1)
                rows_unit(U_PLE, of(pt_hi), of(pt_lo), (0, 1), proj_bank, True, stop=True)
                turn_x(3, 3)
                pe.wait_ge(xt_split, layer * 16 + 16)
                for n in range(4):
                    rows_unit(U_PLE + 1 + n, of(xt_hi), of(xt_lo), (2 * n, 2 * n + 1), acc, n == 0,
                              4 if n == 3 else None)


_INS = ['x', 'p', 'ffn1_norm', 'ffn1_w1', 'ffn1_w3', 'ffn1_w2', 'mix_norm', 'w_in', 'q_norm', 'k_norm',
        'conv_w', 'conv_b', 'lru_wa', 'lru_ba', 'lru_wx', 'lru_bx', 'lru_lambda', 'pool_w', 'pool_scale',
        'w_out', 'ffn2_norm', 'ffn2_w1', 'ffn2_w3', 'ffn2_w2', 'ple_norm', 'ple_gate_w', 'ple_proj']


def kernel(**inputs):
    import concourse.bacc as bacc
    from concourse.bass_utils import run_bass_kernel_spmd

    nc = bacc.Bacc("TRN2", target_bir_lowering=False, num_devices=1)
    arrays, args = {}, []
    for name in _INS:
        a = np.ascontiguousarray(inputs[name])
        arrays[f"in_{name}"] = a
        args.append(nc.dram_tensor(f"in_{name}", a.shape, mybir.dt.from_np(a.dtype), kind="ExternalInput").ap())
    shape = inputs['x'].shape
    args.append(nc.dram_tensor("out_x", shape, F32, kind="ExternalOutput").ap())
    trunk_kernel(nc, *args)
    r = run_bass_kernel_spmd(nc, [arrays], core_ids=[0])
    return r.results[0]["out_x"]
```

```python
from contextlib import ExitStack

import numpy as np

import concourse.bass as bass
from concourse import mybir

P = 128
F32 = mybir.dt.float32
F32R = mybir.dt.float32r
I32 = mybir.dt.int32
ALU = mybir.AluOpType
ACT = mybir.ActivationFunctionType

RING = 3
HALVES = 2
UNIT = 2048
EPS = 1e-6
BANK = 512
WINDOWS = (2, 4, 8, 16)
POOL_SPLITS = (1, 4, 6, 9)


class Steps:

    def __init__(self, engine, semaphore, per_layer):
        self.engine, self.semaphore, self.per_layer = engine, semaphore, per_layer
        self.base, self.count = 0, 0

    def start_layer(self, layer):
        self.base, self.count = layer * self.per_layer, 0

    def done(self, instruction):
        instruction.then_inc(self.semaphore, 1)
        self.count += 1

    def settle(self):
        self.engine.wait_ge(self.semaphore, self.base + self.count)

    def end_layer(self):
        assert self.count == self.per_layer, (self.semaphore, self.count)


def trunk_kernel(nc, x_in, p_in, ffn1_norm, ffn1_w1, ffn1_w3, ffn1_w2, mix_norm, w_in, q_norm, k_norm,
                 conv_w, conv_b, lru_wa, lru_ba, lru_wx, lru_bx, lru_lambda, pool_w, pool_scale,
                 w_out, ffn2_norm, ffn2_w1, ffn2_w3, ffn2_w2, ple_norm, ple_gate_w, ple_proj, out):
    DEPTH, D, FF = ffn1_w1.shape
    SEQ = x_in.shape[1]
    T = SEQ // P
    KC = D // P
    DH = q_norm.shape[1]
    PLE = ple_proj.shape[1]
    TAPS, D_LRU = conv_w.shape[1:]
    D_POOL = pool_scale.shape[1]
    D_SB = D - D_POOL - D_LRU
    HEADS = D_SB // DH
    LC = D_LRU // P
    GROUP = 256
    GROUPS = FF // GROUP
    assert (SEQ, D, DH, PLE, D_SB, D_LRU, D_POOL, TAPS) == (256, 1024, 64, 256, 384, 384, 256, 4)
    assert FF % GROUP == 0 and T == 2

    FFN_UNITS = 3 * GROUPS
    U_FFN1 = 0
    U_MIX = U_FFN1 + FFN_UNITS
    V, QK, XGC, WO = (0, 4), 1, 5, 9
    XGC_COLS = (0, 1, 3, 2)
    WO_ROWS = (3, 0, 1, 2)
    MIX_UNITS = 13
    U_FFN2 = U_MIX + MIX_UNITS
    U_PLE = U_FFN2 + FFN_UNITS
    PLE_UNITS = 5
    UNITS = U_PLE + PLE_UNITS
    assert UNITS % RING == 0
    POOL_UNITS = tuple(U_MIX + n for n in POOL_SPLITS) + (U_PLE + 1,)
    DVE_UNITS = UNITS - len(POOL_UNITS)
    assert not set(POOL_UNITS) & {U_FFN2 - 1, UNITS - 3, UNITS - 2, UNITS - 1}
    USES = UNITS // RING

    ROW_CONV_W = 0
    ROW_CONV_B = ROW_CONV_W + TAPS * LC
    ROW_BA = ROW_CONV_B + LC
    ROW_BX = ROW_BA + LC
    ROW_LAM = ROW_BX + LC
    ROW_SCALE = ROW_LAM + LC
    ROW_QN = ROW_SCALE + D_POOL // P
    ROW_KN = ROW_QN + 1
    ROWS = ROW_KN + 1
    PARAM_DMAS = 10 + 6

    with ExitStack() as ctx:
        def sb(name, shape, dt=F32):
            return ctx.enter_context(nc.sbuf_tensor(name, shape, dt))

        def sem(name):
            return ctx.enter_context(nc.semaphore(name))

        raw = [sb(f"raw{s}", [P, UNIT]) for s in range(RING)]
        whi = [sb(f"w_hi{s}", [P, UNIT], F32R) for s in range(RING)]
        wlo = [sb(f"w_lo{s}", [P, UNIT], F32R) for s in range(RING)]
        x = sb("x", [P, T, D])
        xg = sb("x_gained", [P, T, D])
        xt_hi = sb("xt_hi", [P, KC, SEQ], F32R)
        xt_lo = sb("xt_lo", [P, KC, SEQ], F32R)
        scratch = sb("scratch", [P, 4, BANK])
        gain = [sb(f"gain{i}", [P, D]) for i in range(2)]
        square_sums = sb("square_sums", [P, 4])
        mean_sq = sb("mean_sq", [P, T])
        rms = sb("rms", [P, T])
        rstd = sb("rstd", [P, T])
        ident = sb("ident", [P, P])
        ones = sb("ones", [P, P])
        neg_ones = sb("neg_ones", [P, P])
        neg_later = sb("neg_later", [P, P])
        causal = sb("causal", [P, P])
        head_mean = sb("head_mean", [P, P])
        eps_col = sb("eps_col", [P, 1])
        inv_count = sb("inv_count", [P, 2, SEQ])
        silu = sb("silu", [P, T, GROUP])
        gated = sb("gated", [P, T, GROUP])
        gt_hi = sb("gt_hi", [P, 2, T, P], F32R)
        gt_lo = sb("gt_lo", [P, 2, T, P], F32R)
        param_rows = sb("param_rows", [P, P])
        par = sb("param_cols", [P, ROWS])
        tiny = sb("tiny", [P, 8, LC])
        half_scale = sb("half_scale", [P, LC])
        log_scale = sb("log_scale", [P, LC])
        qk_gain = sb("qk_gain", [P, 1])
        diag = sb("diag_rstd", [P, SEQ])
        rrow = sb("rstd_rows", [P, SEQ])
        qk = sb("qk", [P, 6, SEQ])
        qk_sq = xg[:, :, :].rearrange("p t d -> p (t d)")[:, 0:6 * SEQ].rearrange("p (c n) -> p c n", c=6)
        v = sb("v", [P, T, D_SB])
        HB = 3
        logs = [sb(f"logs{i}", [P, 3 * P]) for i in range(HB)]
        soft = [sb(f"soft{i}", [P, 3 * P]) for i in range(HB)]
        lbeta = [sb(f"lbeta{i}", [P, 3 * P]) for i in range(HB)]
        xpad = sb("xb_padded", [P, LC, TAPS - 1 + SEQ])
        xconv = sb("xconv", [P, LC, SEQ])
        gb = sb("gb", [P, LC, SEQ])
        gates = scratch[:, :, :].rearrange("p q n -> p (q n)")[:, 0:2 * D_LRU // P * SEQ] \
            .rearrange("p (g c n) -> p g c n", g=2, c=LC)
        r_gate, i_gate = gates[:, 0], gates[:, 1]
        th = sb("tanh_half", [P, LC, SEQ])
        rec = sb("rec", [P, LC, SEQ])
        decay = sb("decay", [P, LC, SEQ])
        PADW = max(WINDOWS)
        xc_pad = sb("xc_padded", [P, 2, PADW + SEQ])
        sums = [sb(f"sum{w}", [P, 2, PADW + SEQ]) for w in WINDOWS[:2]]
        sums += [sb(f"sum{w}", [P, 1, PADW + SEQ]) for w in WINDOWS[2:]]
        pooled = sb("pooled", [P, 2, SEQ])
        counts = sb("counts", [P, 2, PADW])
        count_i = pooled[:, :, 0:PADW].bitcast(I32)
        bd_a = sb("bd_a", [P, LC, P])
        bd_x = sb("bd_x", [P, LC, P])
        bd_p = sb("bd_p", [P, 2, P])
        mix_hi = sb("mix_hi", [P, KC, SEQ], F32R)
        mix_lo = sb("mix_lo", [P, KC, SEQ], F32R)
        last_gt_hi, last_gt_lo = (m[:, 2:4, :].rearrange("p c (t n) -> p c t n", t=T) for m in (mix_hi, mix_lo))
        pl = qk[:, 0:T, :]
        pt_hi, pt_lo = mix_hi[:, 0:PLE // P, :], mix_lo[:, 0:PLE // P, :]

        acc = [ctx.enter_context(nc.psum_tensor(f"acc{i}", [P, BANK], F32)) for i in range(4)]
        up = [ctx.enter_context(nc.psum_tensor(f"up{i}", [P, BANK], F32)) for i in range(T)]
        turn = [ctx.enter_context(nc.psum_tensor(f"turn{i}", [P, BANK], F32)) for i in range(2)]

        slot_loaded = [sem(f"slot_loaded{s}") for s in range(RING)]
        hi_split = sem("hi_split")
        lo_split = sem("lo_split")
        pool_split_lo = sem("pool_split_lo")
        unit_used = sem("unit_used")
        x_loaded = [sem(f"x_loaded{t}") for t in range(T)]
        gain_loaded = [sem(f"gain_loaded{i}") for i in range(2)]
        params_loaded = sem("params_loaded")
        p_loaded = sem("p_loaded")
        ident_ready = sem("ident_ready")
        consts_ready = sem("consts_ready")
        pads_ready = sem("pads_ready")
        pool_step = sem("pool_step")
        dve_step = sem("dve_step")
        act_step = sem("act_step")
        acc_ready = sem("acc_ready")
        gained = sem("gained")
        xt_turned = sem("xt_turned")
        xt_rounded = sem("xt_rounded")
        xt_split = sem("xt_split")
        squares_summed = sem("squares_summed")
        mean_ready = sem("mean_ready")
        rms_ready = sem("rms_ready")
        rstd_ready = sem("rstd_ready")
        up_ready = sem("up_ready")
        silu_ready = sem("silu_ready")
        gated_ready = sem("gated_ready")
        g_turned = sem("g_turned")
        gt_rounded = sem("gt_rounded")
        gt_split = sem("gt_split")
        params_turned = sem("params_turned")
        params_ready = sem("params_ready")
        lam_exp_ready = sem("lam_exp_ready")
        diag_ready = sem("diag_ready")
        rrow_turned = sem("rrow_turned")
        rrow_ready = sem("rrow_ready")
        qk_scaled = sem("qk_scaled")
        qk_squared = sem("qk_squared")
        qk_summed = sem("qk_summed")
        qk_rstd = sem("qk_rstd")
        qk_normed = sem("qk_normed")
        v_ready = sem("v_ready")
        z_ready = sem("z_ready")
        log_ready = sem("log_ready")
        keep_ready = sem("keep_ready")
        suffix_ready = sem("suffix_ready")
        logw_ready = sem("logw_ready")
        w_exped = sem("w_exped")
        w_ready = sem("w_ready")
        o_ready = sem("o_ready")
        o_rounded = sem("o_rounded")
        att_split = sem("att_split")
        evacuated = sem("evacuated")
        conv_ready = sem("conv_ready")
        gates_product = sem("gates_product")
        root_ready = sem("root_ready")
        gelu_ready = sem("gelu_ready")
        lru_ready = sem("lru_ready")
        lru_rounded = sem("lru_rounded")
        lru_split = sem("lru_split")
        pooled_ready = sem("pooled_ready")
        pool_product = sem("pool_product")
        pool_rounded = sem("pool_rounded")
        pool_split = sem("pool_split")
        p_turned = sem("p_turned")
        p_rounded = sem("p_rounded")
        p_split = sem("p_split")
        sig_ready = sem("sig_ready")
        scales_ready = sem("scales_ready")
        gates_ready = sem("gates_ready")
        exp_ready = sem("exp_ready")
        inverse_ready = sem("inverse_ready")
        x_ready = sem("x_ready")
        stored = sem("stored")

        block = ctx.enter_context(nc.Block())

        def unit_count(layer, offset, j=0):
            return layer * UNITS + offset + RING * j + 1

        def wait_split(engine, layer, offset, j=0):
            first = offset + RING * (j if isinstance(j, int) else 1)
            before = sum(n < first for n in POOL_UNITS)
            if first in POOL_UNITS:
                engine.wait_ge(pool_split_lo, layer * len(POOL_UNITS) + before + 1)
            else:
                engine.wait_ge(lo_split, layer * DVE_UNITS + offset - before + RING * j + 1 + RING)

        def unit_width(offset):
            return 4 * D_SB if offset - U_MIX in V else UNIT

        def slot_use(layer, offset, j=0):
            return layer * USES + offset // RING + j + 1

        def wait_unit(engine, layer, offset, j=0):
            engine.wait_ge(unit_used, unit_count(layer, offset, j) + RING)

        def wait_quarter(engine, layer, i, q, last_unit):
            if q < 3:
                engine.wait_ge(acc_ready, layer * 12 + 3 * i + q + 1)
            else:
                wait_unit(engine, layer, last_unit)

        def up_product_ready(engine, layer, f, base, j, t):
            if t == 0:
                engine.wait_ge(up_ready, layer * 2 * GROUPS + f * GROUPS + j + 1)
            else:
                first = isinstance(j, int) and j == 0
                wait_unit(engine, layer, base + (1 if first else 0), j)

        PADDED = (param_rows, bd_a, bd_x, bd_p, xpad, xc_pad, *sums)
        PHASE_ENDS = (U_MIX - 1, U_FFN2 - 1, U_PLE - 1, UNITS - 1)
        head_bank = [up[0], up[1], turn[1]]
        out_bank = [turn[0], turn[0], turn[1]]
        proj_bank = [up[0], up[1], turn[0], turn[1]]
        ACT_STEPS, DVE_STEPS, CONSTS = 17, 61, 21

        @block.sync
        def _(sp):
            for t in range(T):
                sp.dma_start(x[:, t, :], x_in[0, t * P:(t + 1) * P, :]).then_inc(x_loaded[t], 16)

            def load(layer, offset, parts, j=0):
                wait_split(sp, layer, offset - RING, j)
                for dst, src in parts:
                    sp.dma_start(dst, src).then_inc(slot_loaded[offset % RING], 16)

            def load_up(layer, offset, half, g, w1, w3, j=0):
                ks = slice(4 * half, 4 * half + 4)
                dst = raw[offset % RING][:, :].rearrange("p (k m n) -> p k m n", k=4, m=2)
                load(layer, offset, [
                    (dst[:, :, m, :], w.rearrange("l (k p) f -> l p k f", p=P)[layer, :, ks, bass.ts(g, GROUP)])
                    for m, w in enumerate((w1, w3))], j)

            def load_rows(layer, offset, w, row0, j=0):
                dst = raw[offset % RING][:, :].rearrange("p (c n) -> p c n", c=2)
                src = w.rearrange("l (r c p) n -> l r p c n", c=2, p=P)
                load(layer, offset, [(dst[:, c, :], src[layer, row0, :, c, :]) for c in (1, 0)], j)

            def load_cols(layer, offset, col0):
                dst = raw[offset % RING][:, :].rearrange("p (k n) -> p k n", k=KC)
                src = w_in.rearrange("l (k p) n -> l p k n", p=P)
                load(layer, offset, [(dst[:, k:k + 4, :], src[layer, :, k:k + 4, col0:col0 + 256])
                                     for k in (4, 0)])

            def load_v(layer, offset, half):
                dst = raw[offset % RING][:, 0:4 * D_SB].rearrange("p (k n) -> p k n", k=4)
                src = w_in.rearrange("l (k p) n -> l p k n", p=P)
                load(layer, offset, [(dst[:, k:k + 2, :],
                                      src[layer, :, 4 * half + k:4 * half + k + 2, 2 * D_SB:3 * D_SB])
                                     for k in (0, 2)])

            def load_gain(layer, i, source):
                sp.dma_start(gain[i % 2][:, :], source[bass.ds(layer, 1), :].to_broadcast([P, D])
                             ).then_inc(gain_loaded[i % 2], 16)

            def load_params(layer):
                sp.wait_ge(pads_ready, len(PADDED))
                for row, src in (
                    (ROW_CONV_W, conv_w.rearrange("l w (c p) -> l (w c) p", p=P)),
                    (ROW_CONV_B, conv_b.rearrange("l (c p) -> l c p", p=P)),
                    (ROW_BA, lru_ba.rearrange("l (c p) -> l c p", p=P)),
                    (ROW_BX, lru_bx.rearrange("l (c p) -> l c p", p=P)),
                    (ROW_LAM, lru_lambda.rearrange("l (c p) -> l c p", p=P)),
                    (ROW_SCALE, pool_scale.rearrange("l (c p) -> l c p", p=P)),
                ):
                    sp.dma_start(param_rows[row:row + src.shape[1], :], src[layer]).then_inc(params_loaded, 16)
                for row, src in ((ROW_QN, q_norm), (ROW_KN, k_norm)):
                    for b in range(2):
                        sp.dma_start(param_rows[row:row + 1, b * DH:(b + 1) * DH],
                                     src[bass.ds(layer, 1), :]).then_inc(params_loaded, 16)
                for bd, src in ((bd_a, lru_wa), (bd_x, lru_wx), (bd_p, pool_w)):
                    for b in range(2):
                        blk = slice(b * DH, (b + 1) * DH)
                        sp.dma_start(bd[blk, :, blk], src.rearrange("l (c b) i j -> l b i c j", b=2)[layer, b]
                                     ).then_inc(params_loaded, 16)

            def load_ffn(layer, base, w1, w3, w2, after_first, before_last):
                load_up(layer, base, 0, 0, w1, w3)
                load_up(layer, base + 1, 1, 0, w1, w3)
                after_first()
                with sp.Fori(1, GROUPS) as j:
                    load_up(layer, base - 1, 0, j, w1, w3, j)
                    load_up(layer, base, 1, j, w1, w3, j)
                    load_rows(layer, base + 1, w2, j - 1, j)
                before_last()
                load_rows(layer, base - 1, w2, GROUPS - 1, GROUPS)

            with sp.Fori(0, DEPTH) as layer:
                load_gain(layer, 0, ffn1_norm)

                def embeddings():
                    sp.dma_start(pl[:, :, :], p_in.rearrange("l b (t p) e -> l p (b t) e", p=P)[layer]
                                 ).then_inc(p_loaded, 16)

                load_ffn(layer, U_FFN1, ffn1_w1, ffn1_w3, ffn1_w2,
                         lambda: load_gain(layer, 1, mix_norm), lambda: load_params(layer))
                load_gain(layer, 2, ffn2_norm)
                load_v(layer, U_MIX + V[0], 0)
                for n in range(3):
                    load_cols(layer, U_MIX + QK + n, 256 * n)
                load_v(layer, U_MIX + V[1], 1)
                for n, part in enumerate(XGC_COLS):
                    load_cols(layer, U_MIX + XGC + n, 3 * D_SB + 256 * part)
                for n, row in enumerate(WO_ROWS):
                    load_rows(layer, U_MIX + WO + n, w_out, row)
                load_gain(layer, 3, ple_norm)
                load_ffn(layer, U_FFN2, ffn2_w1, ffn2_w3, ffn2_w2, lambda: None, embeddings)
                load_rows(layer, U_PLE, ple_proj, 0)
                for n in range(4):
                    load_rows(layer, U_PLE + 1 + n, ple_gate_w, n)
            for q in range(4):
                t, cols = q // 2, slice(q % 2 * BANK, (q % 2 + 1) * BANK)
                sp.wait_ge(x_ready, 4 * DEPTH + q + 1)
                sp.dma_start(out[0, t * P:(t + 1) * P, cols], x[:, t, cols]).then_inc(stored, 16)
            sp.wait_ge(stored, 16 * 4)

        @block.gpsimd
        def _(pool):
            made = [0]

            def link(instruction):
                instruction.then_inc(consts_ready, 1)
                made[0] += 1

            def settle():
                pool.wait_ge(consts_ready, made[0])

            link(nc.gpsimd.memset(ident[:, :], 0.0))
            settle()
            nc.gpsimd.affine_select(out=ident[:, :], in_=ident[:, :], compare_op=ALU.not_equal, fill=1.0,
                                    base=0, pattern=[[-1, P]], channel_multiplier=1).then_inc(ident_ready, 1)
            for tile, value in ((ones, 1.0), (neg_ones, -1.0), (neg_later, -1.0),
                                (causal, 1.0), (head_mean, 0.0), (eps_col, EPS)):
                link(nc.gpsimd.memset(tile[:, :], value))
            for n, w in enumerate(WINDOWS):
                settle()
                blk = slice((n % 2) * DH, (n % 2 + 1) * DH)
                link(nc.gpsimd.memset(inv_count[blk, n // 2, :], 1.0 / w))
            settle()
            link(nc.gpsimd.iota(count_i, pattern=[[0, 2], [1, PADW]], base=1, channel_multiplier=0))
            settle()
            link(nc.gpsimd.tensor_copy(counts[:, :, :], count_i))
            link(nc.gpsimd.affine_select(out=neg_later[:, :], in_=neg_later[:, :], compare_op=ALU.is_gt,
                                         fill=0.0, base=0, pattern=[[-1, P]], channel_multiplier=1))
            link(nc.gpsimd.affine_select(out=causal[:, :], in_=causal[:, :], compare_op=ALU.is_gt,
                                         fill=0.0, base=0, pattern=[[1, P]], channel_multiplier=-1))
            for b in range(P // DH):
                settle()
                blk = slice(b * DH, (b + 1) * DH)
                link(nc.gpsimd.memset(head_mean[blk, blk], 1.0 / DH))
            for n, w in enumerate(WINDOWS):
                settle()
                blk = slice((n % 2) * DH, (n % 2 + 1) * DH)
                link(nc.gpsimd.tensor_scalar(counts[blk, n // 2, :], counts[blk, n // 2, :],
                                             float(w), None, ALU.min))

            settle()
            assert made[0] == CONSTS

            with pool.Fori(0, DEPTH) as layer:
                def split(offset):
                    slot = offset % RING
                    pool.wait_ge(hi_split, unit_count(layer, offset))
                    nc.gpsimd.tensor_tensor(wlo[slot][:, :], raw[slot][:, :], whi[slot][:, :].bitcast(F32),
                                            ALU.subtract).then_inc(pool_split_lo, 1)

                step = Steps(pool, pool_step, 8)
                step.start_layer(layer)
                pool.wait_ge(gain_loaded[0], 16 * (layer * 2 + 1))
                for q in range(4):
                    pool.wait_ge(x_ready, layer * 4 + q + 1)
                    cols = slice(q % 2 * BANK, (q % 2 + 1) * BANK)
                    nc.gpsimd.tensor_tensor(xg[:, q // 2, cols], x[:, q // 2, cols], gain[0][:, cols],
                                            ALU.mult).then_inc(gained, 1)
                for n in POOL_SPLITS:
                    split(U_MIX + n)
                pool.wait_ge(evacuated, layer * 4 + 3)
                pool.wait_ge(inverse_ready, layer + 1)
                pool.wait_ge(pads_ready, len(PADDED))
                source, width = xc_pad, 1
                for n, total in enumerate(sums):
                    chunks = slice(0, 2) if n < 2 else slice(1, 2)
                    here = slice(0, 2) if n < 2 else slice(0, 1)
                    src = source[:, chunks, :] if n <= 2 else source[:, 0:1, :]
                    lo = 2 * width - 1 if n < 3 else PADW
                    step.done(nc.gpsimd.tensor_tensor(total[:, here, lo:], src[:, :, lo:],
                                                      src[:, :, lo - width:PADW + SEQ - width], ALU.add))
                    step.settle()
                    source, width = total, 2 * width
                for n, total in enumerate(sums):
                    blk = slice((n % 2) * DH, (n % 2 + 1) * DH)
                    step.done(nc.gpsimd.tensor_tensor(pooled[blk, n // 2, :], total[blk, 0, PADW:],
                                                      inv_count[blk, n // 2, :], ALU.mult))
                    step.settle()
                nc.gpsimd.tensor_tensor(pooled[:, :, :], pooled[:, :, :], xc_pad[:, :, PADW:],
                                        ALU.subtract).then_inc(pooled_ready, 1)
                split(U_PLE + 1)
                step.end_layer()

        @block.scalar
        def _(act):
            with act.Fori(0, DEPTH) as layer:
                step = Steps(act, act_step, ACT_STEPS)
                step.start_layer(layer)

                def split(offset, j=0):
                    slot = offset % RING
                    width = unit_width(offset)
                    act.wait_ge(slot_loaded[slot], 16 * HALVES * slot_use(layer, offset, j))
                    act.wait_ge(unit_used, unit_count(layer, offset, j))
                    nc.scalar.activation(whi[slot][:, 0:width], raw[slot][:, 0:width], ACT.Copy
                                         ).then_inc(hi_split, 1)

                def square(i, q):
                    t, h = q // 2, q % 2
                    act.wait_ge(gained, layer * 16 + 4 * i + q + 1)
                    last = nc.scalar.activation(scratch[:, q, :], x[:, t, h * BANK:(h + 1) * BANK],
                                                ACT.Square, accum_out=square_sums[:, q:q + 1])
                    if q == 3:
                        last.then_inc(squares_summed, 1)

                def round_xt(i, q):
                    t, h = q // 2, q % 2
                    act.wait_ge(xt_turned, layer * 16 + 4 * i + q + 1)
                    nc.scalar.activation(xt_hi[:, 4 * h:4 * h + 4, t * P:(t + 1) * P],
                                         acc[q][:, :].rearrange("p (k n) -> p k n", k=4),
                                         ACT.Copy).then_inc(xt_rounded, 1)

                def root(i):
                    act.wait_ge(mean_ready, layer * 4 + i + 1)
                    act.wait_ge(consts_ready, CONSTS)
                    nc.scalar.activation(rms[:, :], mean_sq[:, :], ACT.Sqrt, bias=eps_col[:, :],
                                         scale=1.0 / D).then_inc(rms_ready, 1)

                def ffn(f, i, base):
                    def silus(j):
                        for t in range(T):
                            up_product_ready(act, layer, f, base, j, t)
                            nc.scalar.activation(silu[:, t, :], up[t][:, 0:GROUP], ACT.Silu,
                                                 scale=rstd[:, t:t + 1]).then_inc(silu_ready, 1)

                    def round_gt(j, g_hi=gt_hi):
                        act.wait_ge(g_turned, layer * 2 * GROUPS + f * GROUPS + j + 1)
                        nc.scalar.activation(g_hi[:, :, :, :],
                                             turn[0][:, :].rearrange("p (c t n) -> p c t n", c=2, t=T),
                                             ACT.Copy).then_inc(gt_rounded, 1)

                    split(base + 2)
                    act.wait_ge(rstd_ready, layer * 4 + i + 1)
                    silus(0)
                    split(base + 3)
                    round_gt(0)

                    def group(j, g_hi):
                        split(base + 1, j=j)
                        split(base + 2, j=j)
                        act.wait_ge(gated_ready, layer * 4 * GROUPS + (f * GROUPS + j) * 2)
                        silus(j)
                        split(base + 3, j=j)
                        round_gt(j, g_hi)

                    with act.Fori(1, GROUPS - 1) as j:
                        group(j, gt_hi)
                    group(GROUPS - 1, last_gt_hi)

                def params():
                    act.wait_ge(params_turned, layer + 1)
                    nc.scalar.activation(par[:, :], turn[1][:, 0:ROWS], ACT.Copy).then_inc(params_ready, 1)
                    act.wait_ge(params_ready, layer + 1)
                    step.done(nc.scalar.activation(tiny[:, 0, :], par[:, ROW_LAM:ROW_LAM + LC], ACT.Abs))
                    step.settle()
                    nc.scalar.activation(tiny[:, 1, :], tiny[:, 0, :], ACT.Exp, scale=-1.0
                                         ).then_inc(lam_exp_ready, 1)

                round_xt(0, 0)
                split(U_FFN1)
                round_xt(0, 1)
                round_xt(0, 2)
                split(U_FFN1 + 1)
                square(0, 0)
                square(0, 1)
                square(0, 2)
                round_xt(0, 3)
                square(0, 3)
                root(0)
                ffn(0, 0, U_FFN1)
                split(U_MIX + 1)

                square(1, 0)
                square(1, 1)
                round_xt(1, 0)
                round_xt(1, 1)
                square(1, 2)
                round_xt(1, 2)
                split(U_MIX + 2)
                round_xt(1, 3)
                square(1, 3)
                root(1)
                split(U_MIX + 3)
                params()
                split(U_MIX + 4)
                act.wait_ge(rrow_turned, layer + 1)
                nc.scalar.activation(rrow[:, :], turn[1][:, 0:SEQ], ACT.Copy).then_inc(rrow_ready, 1)
                for g in range(3):
                    act.wait_ge(qk_scaled, layer * 3 + g + 1)
                    nc.scalar.activation(qk_sq[:, 2 * g:2 * g + 2, :], qk[:, 2 * g:2 * g + 2, :],
                                         ACT.Square).then_inc(qk_squared, 1)
                    if g < 2:
                        split(U_MIX + 5 + g)
                for g, bank in enumerate((turn[0], turn[1], acc[3])):
                    act.wait_ge(qk_summed, layer * 3 + g + 1)
                    step.done(nc.scalar.activation(qk_sq[:, 2 * g:2 * g + 2, :],
                                                   bank[:, :].rearrange("p (c n) -> p c n", c=2),
                                                   ACT.Ln, bias=eps_col[:, :]))
                step.settle()
                for g in range(3):
                    nc.scalar.activation(qk_sq[:, 2 * g:2 * g + 2, :], qk_sq[:, 2 * g:2 * g + 2, :],
                                         ACT.Exp, scale=-0.5).then_inc(qk_rstd, 1)

                def head_logs(first):
                    for h in range(first, first + HB):
                        act.wait_ge(z_ready, layer * HEADS + h + 1)
                        step.done(nc.scalar.activation(logs[h % HB][:, :], head_bank[h % HB][:, 0:3 * P], ACT.Abs))
                    step.settle()
                    for h in range(first, first + HB):
                        step.done(nc.scalar.activation(logs[h % HB][:, :], logs[h % HB][:, :], ACT.Exp, scale=-1.0))
                    step.settle()
                    for h in range(first, first + HB):
                        nc.scalar.activation(logs[h % HB][:, :], logs[h % HB][:, :], ACT.Ln, bias=ones[:, 0:1]
                                             ).then_inc(log_ready, 1)

                def head_weights(first):
                    for h in range(first, first + HB):
                        act.wait_ge(logw_ready, layer * HEADS + h + 1)
                        nc.scalar.activation(lbeta[h % HB][:, :], lbeta[h % HB][:, :], ACT.Exp
                                             ).then_inc(w_exped, 1)

                def round_o(c):
                    act.wait_ge(o_ready, layer * HEADS + 2 * c + 2)
                    nc.scalar.activation(mix_hi[:, c, :], out_bank[c][:, 0:SEQ], ACT.Copy
                                         ).then_inc(o_rounded, 1)

                def lru_gates():
                    for c in range(LC):
                        act.wait_ge(gates_product, layer * LC + c + 1)
                        nc.scalar.activation(r_gate[:, c, :], acc[c][:, 0:SEQ], ACT.Sigmoid,
                                             bias=par[:, ROW_BA + c:ROW_BA + c + 1])
                        last = nc.scalar.activation(i_gate[:, c, :], acc[c][:, SEQ:2 * SEQ], ACT.Sigmoid,
                                                    bias=par[:, ROW_BX + c:ROW_BX + c + 1])
                    last.then_inc(gates_ready, 1)

                def lru_decay():
                    act.wait_ge(gates_ready, layer + 1)
                    act.wait_ge(scales_ready, layer + 1)
                    for c in range(LC):
                        last = nc.scalar.activation(decay[:, c, :], r_gate[:, c, :], ACT.Exp,
                                                    scale=log_scale[:, c:c + 1])
                    last.then_inc(exp_ready, 1)

                def lru_tanh():
                    for c in range(LC):
                        last = nc.scalar.activation(th[:, c, :], r_gate[:, c, :], ACT.Tanh,
                                                    scale=half_scale[:, c:c + 1])
                    step.done(last)
                    step.settle()

                def lru_root():
                    nc.scalar.activation(r_gate[:, :, :], th[:, :, :], ACT.Sqrt, scale=-1.0
                                         ).then_inc(root_ready, 1)

                def gelu():
                    act.wait_ge(evacuated, layer * 4 + 4)
                    nc.scalar.activation(gb[:, :, :], gb[:, :, :], ACT.Gelu_apprx_tanh).then_inc(gelu_ready, 1)

                def round_pool():
                    act.wait_ge(pool_product, layer + 1)
                    for c in range(2):
                        last = nc.scalar.activation(mix_hi[:, KC - 2 + c, :], acc[3][:, c * SEQ:(c + 1) * SEQ],
                                                    ACT.Copy, scale=par[:, ROW_SCALE + c:ROW_SCALE + c + 1])
                    last.then_inc(pool_rounded, 1)

                def round_lru(c):
                    act.wait_ge(lru_ready, layer * LC + c + 1)
                    nc.scalar.activation(mix_hi[:, 3 + c, :], gb[:, c, :], ACT.Copy).then_inc(lru_rounded, 1)

                split(U_MIX + 7)
                head_logs(0)
                split(U_MIX + 8)
                split(U_MIX + 9)
                head_weights(0)
                split(U_MIX + 10)
                head_logs(3)
                round_o(0)
                lru_gates()
                round_pool()
                split(U_MIX + 11)
                head_weights(3)
                lru_decay()
                lru_tanh()
                round_o(1)
                lru_root()
                round_o(2)
                gelu()
                round_lru(0)
                split(U_MIX + 12)
                round_lru(1)
                round_lru(2)
                split(U_FFN2)
                split(U_FFN2 + 1)

                square(2, 0)
                square(2, 1)
                round_xt(2, 0)
                round_xt(2, 1)
                square(2, 2)
                round_xt(2, 2)
                round_xt(2, 3)
                square(2, 3)
                root(2)
                ffn(1, 2, U_FFN2)
                act.wait_ge(p_turned, layer + 1)
                nc.scalar.activation(pt_hi[:, :, :], turn[1][:, :].rearrange("p (c n) -> p c n", c=2),
                                     ACT.Copy).then_inc(p_rounded, 1)
                split(U_PLE + 1)

                square(3, 0)
                square(3, 1)
                split(U_PLE + 2)
                round_xt(3, 0)
                square(3, 2)
                round_xt(3, 1)
                round_xt(3, 2)
                round_xt(3, 3)
                square(3, 3)
                root(3)
                split(U_PLE + 3)
                split(U_PLE + 4)
                act.wait_ge(rstd_ready, layer * 4 + 4)
                for q in range(4):
                    t = q // 2
                    wait_quarter(act, layer, 3, q, UNITS - 1)
                    nc.scalar.activation(scratch[:, q, :], acc[q][:, :], ACT.Sigmoid,
                                         scale=rstd[:, t:t + 1]).then_inc(sig_ready, 1)
                step.end_layer()

        @block.vector
        def _(dve):
            nc.vector.memset(square_sums[:, 0:1], 0.0).then_inc(lo_split, RING)
            nc.vector.memset(square_sums[:, 1:2], 0.0).then_inc(unit_used, RING)
            for tile in PADDED:
                nc.vector.memset(tile[tuple(slice(None) for _ in tile.shape)], 0.0).then_inc(pads_ready, 1)
            for t in range(T):
                dve.wait_ge(x_loaded[t], 16)
                nc.vector.memset(square_sums[:, 2 + t:3 + t], 0.0).then_inc(x_ready, 2)
            with dve.Fori(0, DEPTH) as layer:
                step = Steps(dve, dve_step, DVE_STEPS)
                step.start_layer(layer)

                def split(offset, j=0):
                    slot = offset % RING
                    width = unit_width(offset)
                    dve.wait_ge(hi_split, unit_count(layer, offset, j))
                    nc.vector.tensor_tensor(wlo[slot][:, 0:width], raw[slot][:, 0:width],
                                            whi[slot][:, 0:width].bitcast(F32), ALU.subtract
                                            ).then_inc(lo_split, 1)

                def quarter(tile, q):
                    return tile[:, q // 2, (q % 2) * BANK:(q % 2 + 1) * BANK]

                def apply_gain(i, q):
                    nc.vector.tensor_tensor(quarter(xg, q), quarter(x, q),
                                            gain[i % 2][:, (q % 2) * BANK:(q % 2 + 1) * BANK],
                                            ALU.mult).then_inc(gained, 1)

                def residual(i, scale, q):
                    if q == 0:
                        dve.wait_ge(gain_loaded[i % 2], 16 * (layer * 2 + i // 2 + 1))
                    wait_quarter(dve, layer, i - 1, q, PHASE_ENDS[i - 1])
                    step.done(nc.vector.scalar_tensor_tensor(
                        out=quarter(x, q), in0=acc[q][:, :], scalar=scale, in1=quarter(x, q),
                        op0=ALU.mult, op1=ALU.add))
                    step.settle()
                    apply_gain(i, q)

                def split_xt(i, q):
                    t, h = q // 2, q % 2
                    dve.wait_ge(xt_rounded, layer * 16 + 4 * i + q + 1)
                    cols = (slice(None), slice(4 * h, 4 * h + 4), slice(t * P, (t + 1) * P))
                    nc.vector.tensor_tensor(xt_lo[cols], acc[q][:, :].rearrange("p (k n) -> p k n", k=4),
                                            xt_hi[cols].bitcast(F32), ALU.subtract).then_inc(xt_split, 1)

                def statistics(i):
                    dve.wait_ge(squares_summed, layer * 4 + i + 1)
                    nc.vector.tensor_tensor(mean_sq[:, :], square_sums[:, 0:4:2], square_sums[:, 1:4:2],
                                            ALU.add).then_inc(mean_ready, 1)
                    dve.wait_ge(rms_ready, layer * 4 + i + 1)
                    nc.vector.reciprocal(rstd[:, :], rms[:, :]).then_inc(rstd_ready, 1)

                def residual_norm(i, scale, next_unit):
                    for q in range(3):
                        residual(i, scale, q)
                    split_xt(i, 0)
                    residual(i, scale, 3)
                    split_xt(i, 1)
                    split_xt(i, 2)
                    if next_unit not in POOL_UNITS:
                        split(next_unit)
                    split_xt(i, 3)

                def ffn(f, i, base):
                    def gates(j):
                        for t in range(T):
                            dve.wait_ge(silu_ready, layer * 4 * GROUPS + (f * GROUPS + j) * 2 + t + 1)
                            nc.vector.scalar_tensor_tensor(
                                out=gated[:, t, :], in0=up[t][:, GROUP:2 * GROUP], scalar=rstd[:, t:t + 1],
                                in1=silu[:, t, :], op0=ALU.mult, op1=ALU.mult).then_inc(gated_ready, 1)

                    def split_gt(j, g_hi=gt_hi, g_lo=gt_lo):
                        dve.wait_ge(gt_rounded, layer * 2 * GROUPS + f * GROUPS + j + 1)
                        nc.vector.tensor_tensor(g_lo[:, :, :, :].rearrange("p c t n -> p (c t n)"), turn[0][:, :],
                                                g_hi[:, :, :, :].bitcast(F32).rearrange("p c t n -> p (c t n)"),
                                                ALU.subtract).then_inc(gt_split, 1)

                    split(base + 2)
                    dve.wait_ge(rstd_ready, layer * 4 + i + 1)
                    gates(0)
                    split(base + 3)
                    split_gt(0)

                    def group(j, g_hi, g_lo):
                        split(base + 1, j=j)
                        split(base + 2, j=j)
                        gates(j)
                        split(base + 3, j=j)
                        split_gt(j, g_hi, g_lo)

                    with dve.Fori(1, GROUPS - 1) as j:
                        group(j, gt_hi, gt_lo)
                    group(GROUPS - 1, last_gt_hi, last_gt_lo)

                def params():
                    dve.wait_ge(lam_exp_ready, layer + 1)
                    e, den, s, s2, poly = (tiny[:, n, :] for n in (1, 2, 3, 4, 5))
                    lam = par[:, ROW_LAM:ROW_LAM + LC]

                    def link(instruction):
                        step.done(instruction)
                        step.settle()

                    link(nc.vector.tensor_scalar(den, e, 2.0, None, ALU.add))
                    link(nc.vector.reciprocal(den, den))
                    link(nc.vector.tensor_tensor(s, e, den, ALU.mult))
                    link(nc.vector.tensor_tensor(s2, s, s, ALU.mult))
                    link(nc.vector.tensor_scalar(poly, s2, 1.0 / 15, None, ALU.mult))
                    for odd in (13, 11, 9, 7, 5, 3):
                        link(nc.vector.scalar_tensor_tensor(out=poly, in0=poly, scalar=1.0 / odd, in1=s2,
                                                            op0=ALU.add, op1=ALU.mult))
                    link(nc.vector.scalar_tensor_tensor(out=poly, in0=poly, scalar=1.0, in1=s,
                                                        op0=ALU.add, op1=ALU.mult))
                    link(nc.vector.tensor_scalar(s, lam, 0.0, 4.0, ALU.min, ALU.mult))
                    link(nc.vector.scalar_tensor_tensor(out=half_scale[:, :], in0=poly, scalar=-8.0, in1=s,
                                                        op0=ALU.mult, op1=ALU.add))
                    nc.vector.tensor_scalar(log_scale[:, :], half_scale[:, :], 2.0, None, ALU.mult
                                            ).then_inc(scales_ready, 1)
                    link(nc.vector.scalar_tensor_tensor(
                        out=qk_gain[:, :], in0=par[:, ROW_QN:ROW_QN + 1], scalar=float(DH) ** -0.5,
                        in1=par[:, ROW_KN:ROW_KN + 1], op0=ALU.mult, op1=ALU.mult))

                split_xt(0, 0)
                split(U_FFN1)
                split_xt(0, 1)
                split_xt(0, 2)
                split(U_FFN1 + 1)
                split_xt(0, 3)
                statistics(0)
                ffn(0, 0, U_FFN1)

                dve.wait_ge(consts_ready, CONSTS)
                dve.wait_ge(pads_ready, len(PADDED))
                nc.vector.reciprocal(inv_count[:, :, 0:PADW], counts[:, :, :]).then_inc(inverse_ready, 1)
                residual_norm(1, 0.5, U_MIX + 1)
                split(U_MIX + 2)
                statistics(1)
                dve.wait_ge(rstd_ready, layer * 4 + 2)
                for t in range(T):
                    last = nc.vector.tensor_scalar(diag[:, t * P:(t + 1) * P], ident[:, :], rstd[:, t:t + 1],
                                                   None, ALU.mult)
                last.then_inc(diag_ready, 1)
                split(U_MIX + 3)
                params()
                rr = rrow[:, :].unsqueeze(1).to_broadcast([P, 2, SEQ])

                def chunks(bank, n=2):
                    return bank[:, :].rearrange("p (c n) -> p c n", c=2)

                dve.wait_ge(rrow_ready, layer + 1)
                for g in range(3):
                    wait_unit(dve, layer, U_MIX + QK + g)
                    nc.vector.tensor_tensor(qk[:, 2 * g:2 * g + 2, :], chunks(acc[g]), rr, ALU.mult
                                            ).then_inc(qk_scaled, 1)
                    if g == 1:
                        split(U_MIX + 5)
                wait_unit(dve, layer, U_MIX + V[1])
                for t in range(T):
                    nc.vector.tensor_scalar(v[:, t, :], up[t][:, 0:D_SB], rstd[:, t:t + 1], None, ALU.mult
                                            ).then_inc(v_ready, 1)
                for g in range(3):
                    dve.wait_ge(qk_rstd, layer * 3 + g + 1)
                    last = nc.vector.tensor_tensor(qk[:, 2 * g:2 * g + 2, :], qk[:, 2 * g:2 * g + 2, :],
                                                   qk_sq[:, 2 * g:2 * g + 2, :], ALU.mult)
                step.done(last)
                step.settle()
                nc.vector.tensor_scalar(qk[:, 0:3, :], qk[:, 0:3, :], qk_gain[:, :], None, ALU.mult
                                        ).then_inc(qk_normed, 1)

                def head_keeps(first):
                    for h in range(first, first + HB):
                        b = h % HB
                        bank = head_bank[b][:, 0:3 * P]
                        dve.wait_ge(log_ready, layer * HEADS + h + 1)
                        if h >= HB:
                            dve.wait_ge(o_ready, layer * HEADS + h - HB + 1)
                        step.done(nc.vector.scalar_tensor_tensor(out=soft[b][:, :], in0=bank, scalar=0.0,
                                                                 in1=logs[b][:, :], op0=ALU.max, op1=ALU.add))
                        step.done(nc.vector.scalar_tensor_tensor(out=lbeta[b][:, :], in0=bank, scalar=0.0,
                                                                 in1=logs[b][:, :], op0=ALU.min, op1=ALU.subtract))
                        step.settle()
                        diagonal = soft[b][:, :].rearrange("p (b c) -> p b c", b=3)[:, 0:3:2, :]
                        nc.vector.tensor_tensor(diagonal, diagonal,
                                                causal[:, :].unsqueeze(1).to_broadcast([P, 2, P]),
                                                ALU.mult).then_inc(keep_ready, 1)

                def mask_weights(first):
                    for h in range(first, first + HB):
                        dve.wait_ge(w_exped, layer * HEADS + h + 1)
                        diagonal = lbeta[h % HB][:, :].rearrange("p (b c) -> p b c", b=3)[:, 0:3:2, :]
                        nc.vector.tensor_tensor(diagonal, diagonal,
                                                causal[:, :].unsqueeze(1).to_broadcast([P, 2, P]),
                                                ALU.mult).then_inc(w_ready, 1)

                def head_sums(first):
                    for h in range(first, first + HB):
                        b = h % HB
                        dve.wait_ge(suffix_ready, layer * HEADS + h + 1)
                        nc.vector.tensor_tensor(lbeta[b][:, :], head_bank[b][:, 0:3 * P], lbeta[b][:, :],
                                                ALU.add).then_inc(logw_ready, 1)

                def split_o(c):
                    dve.wait_ge(o_rounded, layer * 3 + c + 1)
                    nc.vector.tensor_tensor(mix_lo[:, c, :], out_bank[c][:, 0:SEQ], mix_hi[:, c, :].bitcast(F32),
                                            ALU.subtract).then_inc(att_split, 1)

                def evacuate(n, parts):
                    wait_unit(dve, layer, U_MIX + XGC + n)
                    for dst, src, row in parts:
                        last = nc.vector.tensor_tensor(dst, src, row, ALU.mult)
                    last.then_inc(evacuated, 1)

                def convolution():
                    dve.wait_ge(evacuated, layer * 4 + 2)
                    for w in range(TAPS):
                        for c in range(LC):
                            cw = par[:, ROW_CONV_W + w * LC + c:ROW_CONV_W + w * LC + c + 1]
                            window = xpad[:, c, w:w + SEQ]
                            if w == 0:
                                last = nc.vector.tensor_scalar(xconv[:, c, :], window, cw,
                                                               par[:, ROW_CONV_B + c:ROW_CONV_B + c + 1],
                                                               ALU.mult, ALU.add)
                            else:
                                last = nc.vector.scalar_tensor_tensor(
                                    out=xconv[:, c, :], in0=window, scalar=cw, in1=xconv[:, c, :],
                                    op0=ALU.mult, op1=ALU.add)
                            if w < TAPS - 1:
                                step.done(last)
                        if w < TAPS - 1:
                            step.settle()
                    last.then_inc(conv_ready, 1)

                def split_lru(c):
                    dve.wait_ge(lru_rounded, layer * LC + c + 1)
                    nc.vector.tensor_tensor(mix_lo[:, 3 + c, :], gb[:, c, :], mix_hi[:, 3 + c, :].bitcast(F32),
                                            ALU.subtract).then_inc(lru_split, 1)

                def gated_input():
                    dve.wait_ge(gates_ready, layer + 1)
                    step.done(nc.vector.tensor_tensor(i_gate[:, :, :], i_gate[:, :, :], xconv[:, :, :], ALU.mult))

                def recurrence():
                    dve.wait_ge(exp_ready, layer + 1)
                    dve.wait_ge(root_ready, layer + 1)
                    step.done(nc.vector.scalar_tensor_tensor(out=rec[:, :, :], in0=decay[:, :, :], scalar=1.0,
                                                             in1=r_gate[:, :, :], op0=ALU.add, op1=ALU.mult))
                    step.settle()
                    for c in range(LC):
                        step.done(nc.vector.tensor_tensor(rec[:, c, :], rec[:, c, :], i_gate[:, c, :], ALU.mult))
                        step.settle()
                        step.done(nc.vector.tensor_tensor_scan(th[:, c, :], decay[:, c, :], rec[:, c, :], 0.0,
                                                               ALU.mult, ALU.add))
                        step.settle()
                        dve.wait_ge(gelu_ready, layer + 1)
                        nc.vector.tensor_tensor(gb[:, c, :], gb[:, c, :], th[:, c, :], ALU.mult
                                                ).then_inc(lru_ready, 1)
                        if c > 0:
                            split_lru(c - 1)
                        else:
                            split_o(2)
                    split_lru(LC - 1)

                def split_pool():
                    dve.wait_ge(pool_rounded, layer + 1)
                    for c in range(2):
                        last = nc.vector.scalar_tensor_tensor(
                            out=mix_lo[:, KC - 2 + c, :], in0=acc[3][:, c * SEQ:(c + 1) * SEQ],
                            scalar=par[:, ROW_SCALE + c:ROW_SCALE + c + 1],
                            in1=mix_hi[:, KC - 2 + c, :].bitcast(F32), op0=ALU.mult, op1=ALU.subtract)
                    last.then_inc(pool_split, 1)

                split(U_MIX + 7)
                head_keeps(0)
                evacuate(0, [(xpad[:, 0:2, TAPS - 1:], chunks(acc[0]), rr)])
                split(U_MIX + 8)
                evacuate(1, [(xpad[:, 2, TAPS - 1:], acc[1][:, 0:SEQ], rrow[:, :]),
                             (gb[:, 0, :], acc[1][:, SEQ:2 * SEQ], rrow[:, :])])
                head_sums(0)
                evacuate(2, [(xc_pad[:, :, PADW:], chunks(acc[2]), rr)])
                convolution()
                mask_weights(0)
                evacuate(3, [(gb[:, 1:3, :], chunks(acc[3]), rr)])
                split(U_MIX + 10)
                split_o(0)
                head_keeps(3)
                split_pool()
                head_sums(3)
                mask_weights(3)
                gated_input()
                split(U_MIX + 11)
                split_o(1)
                recurrence()
                split(U_MIX + 12)
                split(U_FFN2)

                residual_norm(2, 1.0, U_FFN2 + 1)
                statistics(2)
                ffn(1, 2, U_FFN2)
                dve.wait_ge(p_rounded, layer + 1)
                nc.vector.tensor_tensor(pt_lo[:, :, :], chunks(turn[1]), pt_hi[:, :, :].bitcast(F32),
                                        ALU.subtract).then_inc(p_split, 1)

                residual_norm(3, 0.5, U_PLE + 1)
                split(U_PLE + 2)
                statistics(3)
                split(U_PLE + 3)
                split(U_PLE + 4)
                for q in range(4):
                    dve.wait_ge(sig_ready, layer * 4 + q + 1)
                    step.done(nc.vector.tensor_tensor(scratch[:, q, :], proj_bank[q][:, :], scratch[:, q, :],
                                                      ALU.mult))
                    step.settle()
                    nc.vector.tensor_tensor(quarter(x, q), quarter(x, q), scratch[:, q, :], ALU.add
                                            ).then_inc(x_ready, 1)
                dve.wait_ge(x_ready, 4 * layer + 8)
                step.end_layer()

        @block.tensor
        def _(pe):
            pe.wait_ge(ident_ready, 1)
            with pe.Fori(0, DEPTH) as layer:
                def unit_split(offset, j=0):
                    wait_split(pe, layer, offset, j)

                def three(bank, a_hi, a_lo, b_hi, b_lo, start, stop):
                    nc.tensor.matmul(bank, a_hi, b_hi, start=start, stop=False)
                    nc.tensor.matmul(bank, a_hi, b_lo, start=False, stop=False)
                    return nc.tensor.matmul(bank, a_lo, b_hi, start=False, stop=stop)

                def turn_x(i, q):
                    t, h = q // 2, q % 2
                    pe.wait_ge(gained, layer * 16 + 4 * i + q + 1)
                    for k in range(4):
                        last = nc.tensor.transpose(acc[q][:, k * P:(k + 1) * P],
                                                   xg[:, t, (4 * h + k) * P:(4 * h + k + 1) * P], ident[:, :])
                    last.then_inc(xt_turned, 1)

                def xt_wait(i, half, t):
                    pe.wait_ge(xt_split, layer * 16 + 4 * i + 2 * t + half + 1)

                def rows_unit(offset, a_hi, a_lo, chunks, banks, first=False, last_of=None, j=0, stop=False,
                              before={}):
                    slot = offset % RING
                    unit_split(offset, j)
                    ends = last_of is not None
                    order = [(c, t, h) for c in range(2) for t in range(T) for h in range(2)]
                    if ends:
                        order.sort(key=lambda x: (2 * x[1] + x[2], x[0]))
                    for c, t, h in order:
                        q = 2 * t + h
                        if ends and last_of < 4 and (q, c) == (3, 0):
                            turn_x(last_of, 0)
                        if (c, q) in before:
                            before[c, q]()
                        cols = slice(c * D + h * BANK, c * D + (h + 1) * BANK)
                        last = three(banks[q][:, :], a_hi(chunks[c], t), a_lo(chunks[c], t),
                                     whi[slot][:, cols], wlo[slot][:, cols],
                                     start=first and c == 0, stop=(ends or stop) and c == 1)
                        if ends and c == 1 and q < 3:
                            last.then_inc(acc_ready, 1)
                    last.then_inc(unit_used, 1)
                    if ends and last_of < 4:
                        turn_x(last_of, 1)
                        turn_x(last_of, 2)

                def of(tile):
                    return lambda k, t: tile[:, k, t * P:(t + 1) * P]

                def ffn(f, i, base, before_last):
                    def up_group(offset, j, norm=None, start_after=None):
                        for half in range(2):
                            o = offset + half
                            slot = o % RING
                            early = norm is not None and half == 0
                            if early:
                                pe.wait_ge(hi_split, unit_count(layer, o, j))
                            else:
                                unit_split(o, j)
                            for t in range(T):
                                if norm is not None:
                                    if (half, t) == (0, 1):
                                        turn_x(norm, 3)
                                    xt_wait(norm, half, t)
                                if start_after is not None and half == 0:
                                    pe.wait_ge(gated_ready, layer * 4 * GROUPS + f * 2 * GROUPS + t + 1)
                                if early and t == 0:
                                    for a in (xt_hi, xt_lo):
                                        for k in range(4):
                                            cols = slice(k * BANK, (k + 1) * BANK)
                                            nc.tensor.matmul(up[t][:, :], of(a)(k, t), whi[slot][:, cols],
                                                             start=a is xt_hi and k == 0, stop=False)
                                    unit_split(o, j)
                                    for k in range(4):
                                        cols = slice(k * BANK, (k + 1) * BANK)
                                        nc.tensor.matmul(up[t][:, :], of(xt_hi)(k, t), wlo[slot][:, cols],
                                                         start=False, stop=False)
                                    continue
                                for kk in range(4):
                                    k = 4 * half + kk
                                    cols = slice(kk * BANK, (kk + 1) * BANK)
                                    last = three(up[t][:, :], of(xt_hi)(k, t), of(xt_lo)(k, t),
                                                 whi[slot][:, cols], wlo[slot][:, cols],
                                                 start=k == 0, stop=k == KC - 1)
                                if half == 1 and t == 0:
                                    last.then_inc(up_ready, 1)
                            last.then_inc(unit_used, 1)
                            if half == 0 and start_after is not None:
                                start_after()

                    def turn_g(g):
                        pe.wait_ge(gated_ready, layer * 4 * GROUPS + (f * GROUPS + g) * 2 + 2)
                        for c in range(2):
                            for t in range(T):
                                last = nc.tensor.transpose(turn[0][:, (c * T + t) * P:(c * T + t + 1) * P],
                                                           gated[:, t, c * P:(c + 1) * P], ident[:, :])
                        last.then_inc(g_turned, 1)

                    def down(offset, j, g, first, last_of=None, g_hi=gt_hi, g_lo=gt_lo, before={}):
                        pe.wait_ge(gt_split, layer * 2 * GROUPS + f * GROUPS + g + 1)
                        rows_unit(offset, lambda c, t: g_hi[:, c, t, :], lambda c, t: g_lo[:, c, t, :],
                                  (0, 1), acc, first, last_of, j, before=before)

                    up_group(base, 0, i)
                    up_group(base - 1, 1, start_after=lambda: turn_g(0))
                    down(base + 1, 1, 0, True)
                    turn_g(1)
                    with pe.Fori(2, GROUPS - 1) as j:
                        up_group(base - 1, j)
                        down(base + 1, j, j - 1, False)
                        turn_g(j)
                    last_group = GROUPS - 1
                    up_group(base - 1, last_group)
                    down(base + 1, last_group, last_group - 1, False,
                         before={(1, 0): lambda: turn_g(last_group)})
                    before_last()
                    down(base - 1, GROUPS, last_group, False, i + 1, last_gt_hi, last_gt_lo)

                def turn_params():
                    pe.wait_ge(consts_ready, CONSTS)
                    pe.wait_ge(params_loaded, 16 * PARAM_DMAS * (layer + 1))
                    nc.tensor.transpose(turn[1][:, 0:P], param_rows[:, :], ident[:, :]
                                        ).then_inc(params_turned, 1)

                def turn_p():
                    pe.wait_ge(p_loaded, 16 * (layer + 1))
                    for c in range(2):
                        for t in range(T):
                            last = nc.tensor.transpose(turn[1][:, (c * T + t) * P:(c * T + t + 1) * P],
                                                       pl[:, t, c * P:(c + 1) * P], ident[:, :])
                    last.then_inc(p_turned, 1)

                for q in range(3):
                    turn_x(0, q)
                ffn(0, 0, U_FFN1, turn_params)

                def features(n, bank, between=None):
                    slot = (U_MIX + n) % RING
                    unit_split(U_MIX + n)
                    for c in range(2):
                        if c == 1 and between is not None:
                            between()
                        out_ = bank[:, c * SEQ:(c + 1) * SEQ]
                        for k in range(KC):
                            cols = slice(k * 256 + c * P, k * 256 + (c + 1) * P)
                            nc.tensor.matmul(out_, whi[slot][:, cols], xt_hi[:, k, :], start=k == 0, stop=False)
                            nc.tensor.matmul(out_, whi[slot][:, cols], xt_lo[:, k, :], start=False, stop=False)
                            last = nc.tensor.matmul(out_, wlo[slot][:, cols], xt_hi[:, k, :], start=False,
                                                    stop=k == KC - 1)
                    last.then_inc(unit_used, 1)

                def head_z(h):
                    if h == 0:
                        pe.wait_ge(qk_normed, layer + 1)
                        pe.wait_ge(v_ready, layer * T + T)
                    if h >= HB:
                        pe.wait_ge(logw_ready, layer * HEADS + h - HB + 1)
                    rows, c, bank = slice(h % 2 * DH, (h % 2 + 1) * DH), h // 2, head_bank[h % HB]
                    nc.tensor.matmul(bank[:, 0:2 * P], qk[rows, 3 + c, 0:P], qk[rows, c, :], start=True, stop=True)
                    nc.tensor.matmul(bank[:, 2 * P:3 * P], qk[rows, 3 + c, P:2 * P], qk[rows, c, P:2 * P],
                                     start=True, stop=True).then_inc(z_ready, 1)

                def head_suffix(h):
                    pe.wait_ge(keep_ready, layer * HEADS + h + 1)
                    bank = head_bank[h % HB]
                    nc.tensor.matmul(bank[:, 0:3 * P], neg_later[:, :], soft[h % HB][:, :], start=True, stop=False)
                    nc.tensor.matmul(bank[:, P:2 * P], neg_ones[:, :], soft[h % HB][:, 2 * P:3 * P],
                                     start=False, stop=True).then_inc(suffix_ready, 1)

                def lru_gate_products():
                    pe.wait_ge(conv_ready, layer + 1)
                    for c in range(LC):
                        nc.tensor.matmul(acc[c][:, 0:SEQ], bd_a[:, c, :], xconv[:, c, :], start=True, stop=True)
                        nc.tensor.matmul(acc[c][:, SEQ:2 * SEQ], bd_x[:, c, :], xconv[:, c, :],
                                         start=True, stop=True).then_inc(gates_product, 1)

                def pool_products():
                    pe.wait_ge(pooled_ready, layer + 1)
                    pe.wait_ge(evacuated, layer * 4 + 4)
                    for c in range(2):
                        last = nc.tensor.matmul(acc[3][:, c * SEQ:(c + 1) * SEQ], bd_p[:, c, :],
                                                pooled[:, c, :], start=True, stop=True)
                    last.then_inc(pool_product, 1)

                def head_out(h):
                    pe.wait_ge(w_ready, layer * HEADS + h + 1)
                    if h == 2:
                        pe.wait_ge(att_split, layer * 3 + 1)
                    rows, cols = slice(h % 2 * DH, (h % 2 + 1) * DH), slice(h * DH, (h + 1) * DH)
                    nc.tensor.matmul(out_bank[h // 2][rows, 0:2 * P], v[:, 0, cols], lbeta[h % HB][:, 0:2 * P],
                                     start=True, stop=False)
                    nc.tensor.matmul(out_bank[h // 2][rows, P:2 * P], v[:, 1, cols], lbeta[h % HB][:, 2 * P:3 * P],
                                     start=False, stop=True).then_inc(o_ready, 1)

                def values(half):
                    slot = (U_MIX + V[half]) % RING
                    unit_split(U_MIX + V[half])
                    for t in range(T):
                        if half == 0:
                            if t == 1:
                                turn_x(1, 3)
                            xt_wait(1, 0, t)
                        for kk in range(4):
                            k = 4 * half + kk
                            cols = slice(kk * D_SB, (kk + 1) * D_SB)
                            last = three(up[t][:, 0:D_SB], of(xt_hi)(k, t), of(xt_lo)(k, t),
                                         whi[slot][:, cols], wlo[slot][:, cols], start=k == 0, stop=k == KC - 1)
                    last.then_inc(unit_used, 1)

                def head_means(g, bank):
                    pe.wait_ge(qk_squared, layer * 3 + g + 1)
                    nc.tensor.matmul(bank[:, :], head_mean[:, :], qk_sq[:, 2 * g:2 * g + 2, :],
                                     start=True, stop=True).then_inc(qk_summed, 1)

                def three_heads(part, first):
                    for h in range(first, first + HB):
                        part(h)

                values(0)
                xt_wait(1, 1, 1)
                features(QK, acc[0])
                pe.wait_ge(diag_ready, layer + 1)
                pe.wait_ge(params_ready, layer + 1)
                nc.tensor.matmul(turn[1][:, 0:SEQ], ones[:, :], diag[:, :], start=True, stop=True
                                 ).then_inc(rrow_turned, 1)
                features(QK + 1, acc[1])
                features(QK + 2, acc[2])
                head_means(0, turn[0])
                pe.wait_ge(rrow_ready, layer + 1)
                head_means(1, turn[1])
                values(1)
                head_means(2, acc[3])
                features(XGC, acc[0])
                three_heads(head_z, 0)
                features(XGC + 1, acc[1])
                features(XGC + 2, acc[2], lambda: three_heads(head_suffix, 0))
                features(XGC + 3, acc[3], lambda: three_heads(head_z, 3))
                head_out(0)
                head_out(1)
                lru_gate_products()
                head_out(2)
                pool_products()
                three_heads(head_suffix, 3)
                pe.wait_ge(gates_ready, layer + 1)
                pe.wait_ge(pool_split, layer + 1)
                rows_unit(U_MIX + WO, of(mix_hi), of(mix_lo), (6, 7), acc, True)
                three_heads(head_out, 3)
                for n, row in enumerate(WO_ROWS):
                    if n == 0:
                        continue
                    if row == 0:
                        pe.wait_ge(att_split, layer * 3 + 2)
                    else:
                        pe.wait_ge(lru_split, layer * LC + (1 if row == 1 else LC))
                        if row == 1:
                            pe.wait_ge(att_split, layer * 3 + 3)
                    rows_unit(U_MIX + WO + n, of(mix_hi), of(mix_lo), (2 * row, 2 * row + 1), acc, False,
                              2 if n == 3 else None)

                ffn(1, 2, U_FFN2, turn_p)

                pe.wait_ge(p_split, layer + 1)
                rows_unit(U_PLE, of(pt_hi), of(pt_lo), (0, 1), proj_bank, True, stop=True,
                          before={(1, 1): lambda: turn_x(3, 3)})
                xt_wait(3, 0, 1)
                for n in range(4):
                    rows_unit(U_PLE + 1 + n, of(xt_hi), of(xt_lo), (2 * n, 2 * n + 1), acc, n == 0,
                              4 if n == 3 else None,
                              before={(0, 3): lambda: xt_wait(3, 1, 1)} if n == 0 else {})


_INS = ['x', 'p', 'ffn1_norm', 'ffn1_w1', 'ffn1_w3', 'ffn1_w2', 'mix_norm', 'w_in', 'q_norm', 'k_norm',
        'conv_w', 'conv_b', 'lru_wa', 'lru_ba', 'lru_wx', 'lru_bx', 'lru_lambda', 'pool_w', 'pool_scale',
        'w_out', 'ffn2_norm', 'ffn2_w1', 'ffn2_w3', 'ffn2_w2', 'ple_norm', 'ple_gate_w', 'ple_proj']


def kernel(**inputs):
    import concourse.bacc as bacc
    from concourse.bass_utils import run_bass_kernel_spmd

    nc = bacc.Bacc("TRN2", target_bir_lowering=False, num_devices=1)
    arrays, args = {}, []
    for name in _INS:
        a = np.ascontiguousarray(inputs[name])
        arrays[f"in_{name}"] = a
        args.append(nc.dram_tensor(f"in_{name}", a.shape, mybir.dt.from_np(a.dtype), kind="ExternalInput").ap())
    shape = inputs['x'].shape
    args.append(nc.dram_tensor("out_x", shape, F32, kind="ExternalOutput").ap())
    trunk_kernel(nc, *args)
    r = run_bass_kernel_spmd(nc, [arrays], core_ids=[0])
    return r.results[0]["out_x"]
```
